# Optimizing a Trainium2 kernel written in Bass

```python
import jax, jax.numpy as jnp
from jax import lax
import numpy as np
import math
import jax
import jax.numpy as jnp

D_MODEL = 1024
BATCH = 1
SEQ = 512
DEPTH = 2

N_MIXERS = 2
RMS_EPS = 1e-6
L2_EPS = 1e-6

GDN_HEADS = 8
GDN_DK = 128
GDN_DV = 128
GDN_CONV = 4
GDN_CHUNK = 64
GDN_QK_WIDTH = GDN_HEADS * GDN_DK
GDN_V_WIDTH = GDN_HEADS * GDN_DV
GDN_IN_WIDTH = 2 * GDN_QK_WIDTH + 2 * GDN_V_WIDTH + 2 * GDN_HEADS

DIL_GROUPS = ((128, 1), (512, 4), (2048, 16))
N_DIL_GROUPS = 3
DIL_HEADS_PER_GROUP = 8
DIL_HEAD_DIM = 64
DIL_TOTAL_HEADS = N_DIL_GROUPS * DIL_HEADS_PER_GROUP
DIL_IN_WIDTH = 3 * DIL_TOTAL_HEADS * DIL_HEAD_DIM
DIL_OUT_WIDTH = DIL_HEADS_PER_GROUP * DIL_HEAD_DIM
ALIBI_MAX_BIAS = 8.0

FFN_HIDDEN = -(-8 * D_MODEL // (3 * 256)) * 256


def _rmsnorm(x, w):
    xf = x.astype(jnp.float32)
    y = xf * lax.rsqrt(jnp.mean(xf * xf, axis=-1, keepdims=True) + RMS_EPS)
    return (y * w.astype(jnp.float32)).astype(x.dtype)

def _l2norm(x):
    xf = x.astype(jnp.float32)
    return xf * lax.rsqrt(jnp.sum(xf * xf, axis=-1, keepdims=True) + L2_EPS)

def _causal_depthwise_conv(x, w):
    c = x.shape[-1]
    return lax.conv_general_dilated(
        x, w[:, None, :].astype(x.dtype), window_strides=(1,),
        padding=[(w.shape[0] - 1, 0)], dimension_numbers=("NWC", "WIO", "NWC"),
        feature_group_count=c)

def _chunk_gated_delta_rule(q, k, v, g, beta):
    b, s, h, dk = q.shape
    dv = v.shape[-1]
    c = GDN_CHUNK
    nc = s // c

    def chunks(t):
        return t.reshape(b, nc, c, h, -1).transpose(0, 3, 1, 2, 4)

    q, k, v = chunks(q), chunks(k), chunks(v)
    g = g.reshape(b, nc, c, h).transpose(0, 3, 1, 2)
    beta = beta.reshape(b, nc, c, h).transpose(0, 3, 1, 2)
    gc = jnp.cumsum(g, axis=-1)
    idx = jnp.arange(c)
    causal = idx[:, None] >= idx[None, :]
    strict = idx[:, None] > idx[None, :]
    decay = jnp.exp(jnp.where(causal, gc[..., :, None] - gc[..., None, :], -jnp.inf))
    kk = jnp.einsum("bhncd,bhnmd->bhncm", k, k)
    a_mat = jnp.where(strict, kk * beta[..., :, None] * decay, 0.0) + jnp.eye(c, dtype=jnp.float32)
    rhs = jnp.concatenate([v * beta[..., None], k * (beta * jnp.exp(gc))[..., None]], axis=-1)
    sol = lax.linalg.triangular_solve(a_mat, rhs, left_side=True, lower=True, unit_diagonal=True)
    u, w = sol[..., :dv], sol[..., dv:]
    qk = jnp.einsum("bhncd,bhnmd->bhncm", q, k) * decay
    q_dec = q * jnp.exp(gc)[..., None]
    k_tail = k * jnp.exp(gc[..., -1:] - gc)[..., None]
    c_dec = jnp.exp(gc[..., -1])
    xs = (jnp.moveaxis(qk, 2, 0), jnp.moveaxis(q_dec, 2, 0), jnp.moveaxis(k_tail, 2, 0),
          jnp.moveaxis(u, 2, 0), jnp.moveaxis(w, 2, 0), jnp.moveaxis(c_dec, 2, 0))

    def step(state, inp):
        qk_c, qd_c, kt_c, u_c, w_c, cd_c = inp
        v_new = u_c - jnp.einsum("bhck,bhkv->bhcv", w_c, state)
        o_c = (jnp.einsum("bhck,bhkv->bhcv", qd_c, state)
               + jnp.einsum("bhcm,bhmv->bhcv", qk_c, v_new))
        state = state * cd_c[..., None, None] + jnp.einsum("bhck,bhcv->bhkv", kt_c, v_new)
        return state, o_c

    s0 = jnp.zeros((b, h, dk, dv), jnp.float32)
    _, o = lax.scan(step, s0, xs)
    return o.transpose(1, 0, 3, 2, 4).reshape(b, s, h, dv)

def _gated_deltanet(h, w_in, conv_w, a_log, dt_bias, norm_w, w_out):
    b, s, _ = h.shape
    proj = h @ w_in
    n_qkv = 2 * GDN_QK_WIDTH + GDN_V_WIDTH
    qkv = jax.nn.silu(_causal_depthwise_conv(proj[..., :n_qkv], conv_w))
    z = proj[..., n_qkv:n_qkv + GDN_V_WIDTH].reshape(b, s, GDN_HEADS, GDN_DV)
    a = proj[..., n_qkv + GDN_V_WIDTH:n_qkv + GDN_V_WIDTH + GDN_HEADS].astype(jnp.float32)
    bb = proj[..., n_qkv + GDN_V_WIDTH + GDN_HEADS:].astype(jnp.float32)
    q = _l2norm(qkv[..., :GDN_QK_WIDTH].reshape(b, s, GDN_HEADS, GDN_DK)) * (GDN_DK ** -0.5)
    k = _l2norm(qkv[..., GDN_QK_WIDTH:2 * GDN_QK_WIDTH].reshape(b, s, GDN_HEADS, GDN_DK))
    v = qkv[..., 2 * GDN_QK_WIDTH:].reshape(b, s, GDN_HEADS, GDN_DV).astype(jnp.float32)
    beta = jax.nn.sigmoid(bb)
    g = -jnp.exp(a_log.astype(jnp.float32)) * jax.nn.softplus(a + dt_bias.astype(jnp.float32))
    o = _chunk_gated_delta_rule(q, k, v, g, beta)
    o = o * lax.rsqrt(jnp.mean(o * o, axis=-1, keepdims=True) + RMS_EPS)
    o = o * norm_w.astype(jnp.float32) * jax.nn.silu(z.astype(jnp.float32))
    return o.astype(h.dtype).reshape(b, s, GDN_V_WIDTH) @ w_out

def _dilated_group_attention(q, k, v, slopes, dilation, span):
    b, s, h, dh = q.shape
    n_sub = -(-s // dilation)
    nb = -(-n_sub // span)
    l_pad = nb * span
    t_pad = l_pad * dilation

    def to_blocks(t):
        t = jnp.pad(t, ((0, 0), (0, t_pad - s), (0, 0), (0, 0)))
        t = t.reshape(b, l_pad, dilation, h, dh).transpose(0, 2, 1, 3, 4)
        return t.reshape(b, dilation, nb, span, h, dh)

    def with_prev(t):
        prev = jnp.pad(t, ((0, 0), (0, 0), (1, 0), (0, 0), (0, 0), (0, 0)))[:, :, :-1]
        return jnp.concatenate([prev, t], axis=3)

    def from_blocks(t):
        e = t.shape[-1]
        t = t.reshape(b, dilation, l_pad, h, e).transpose(0, 2, 1, 3, 4)
        return t.reshape(b, t_pad, h, e)[:, :s]

    qb = to_blocks(q)
    kb = with_prev(to_blocks(k))
    vb = with_prev(to_blocks(v))
    scores = jnp.einsum("brnqhd,brnkhd->brnhqk", qb, kb,
                        preferred_element_type=jnp.float32) * (dh ** -0.5)
    qi = jnp.arange(span)
    kj = jnp.arange(2 * span)
    steps = qi[:, None] + span - kj[None, :]
    key_sub = jnp.arange(nb)[:, None] * span - span + kj[None, :]
    valid = ((steps >= 0) & (steps <= span))[None] & (key_sub >= 0)[:, None, :]
    bias = -slopes.astype(jnp.float32)[:, None, None] * (steps * dilation).astype(jnp.float32)
    logits = jnp.where(valid[:, None], scores + bias, -jnp.inf)
    m = jnp.max(logits, axis=-1, keepdims=True)
    p = jnp.exp(logits - m)
    l = jnp.sum(p, axis=-1)
    o = jnp.einsum("brnhqk,brnkhd->brnqhd", p, vb.astype(jnp.float32))
    o = o / l.transpose(0, 1, 2, 4, 3)[..., None]
    m_out = from_blocks(m[..., 0].transpose(0, 1, 2, 4, 3)[..., None])[..., 0]
    l_out = from_blocks(l.transpose(0, 1, 2, 4, 3)[..., None])[..., 0]
    return from_blocks(o), m_out, l_out

def _dilated_attention(h, w_in, q_norm, k_norm, w_out):
    b, s, _ = h.shape
    qkv = (h @ w_in).reshape(b, s, 3, N_DIL_GROUPS, DIL_HEADS_PER_GROUP, DIL_HEAD_DIM)
    q = _rmsnorm(qkv[:, :, 0], q_norm)
    k = _rmsnorm(qkv[:, :, 1], k_norm)
    v = qkv[:, :, 2]
    slopes = (2.0 ** (-ALIBI_MAX_BIAS * jnp.arange(1, DIL_TOTAL_HEADS + 1, dtype=jnp.float32)
                      / DIL_TOTAL_HEADS)).reshape(N_DIL_GROUPS, DIL_HEADS_PER_GROUP)
    outs, maxes, dens = [], [], []
    for gi, (window, dilation) in enumerate(DIL_GROUPS):
        o_g, m_g, l_g = _dilated_group_attention(q[:, :, gi], k[:, :, gi], v[:, :, gi],
                                                 slopes[gi], dilation, window // dilation)
        outs.append(o_g)
        maxes.append(m_g)
        dens.append(l_g)
    o_all = jnp.stack(outs)
    m_all = jnp.stack(maxes)
    l_all = jnp.stack(dens)
    wts = l_all * jnp.exp(m_all - jnp.max(m_all, axis=0, keepdims=True))
    o = jnp.sum(wts[..., None] * o_all, axis=0) / jnp.sum(wts, axis=0)[..., None]
    return o.astype(h.dtype).reshape(b, s, DIL_OUT_WIDTH) @ w_out

def _swiglu(h, w_in, w_out):
    gu = h @ w_in
    return (jax.nn.silu(gu[..., :FFN_HIDDEN]) * gu[..., FFN_HIDDEN:]) @ w_out

def first_inputs(seed: int = 0) -> dict:
    key = jax.random.key(seed)
    ks = jax.random.split(key, 16)
    f32 = jnp.float32
    n_a = (DEPTH + 1) // 2
    n_b = DEPTH // 2
    out_scale = (2.0 * DEPTH) ** -0.5

    def nrm(k, shape, scale):
        return jax.random.normal(k, shape, f32) * scale

    def gain(k, shape):
        return 1.0 + 0.02 * jax.random.normal(k, shape, f32)

    dt = jnp.exp(jax.random.uniform(ks[6], (n_a, GDN_HEADS), f32, np.log(1e-3), np.log(1e-1)))
    return {
        "x": nrm(ks[0], (BATCH, SEQ, D_MODEL), 1.0),
        "norm_mix": gain(ks[1], (DEPTH, D_MODEL)),
        "norm_ffn": gain(ks[2], (DEPTH, D_MODEL)),
        "gdn_w_in": nrm(ks[3], (n_a, D_MODEL, GDN_IN_WIDTH), D_MODEL ** -0.5),
        "gdn_conv_w": nrm(ks[4], (n_a, GDN_CONV, 2 * GDN_QK_WIDTH + GDN_V_WIDTH), GDN_CONV ** -0.5),
        "gdn_a_log": jnp.log(jax.random.uniform(ks[5], (n_a, GDN_HEADS), f32, 1.0, 16.0)),
        "gdn_dt_bias": dt + jnp.log(-jnp.expm1(-dt)),
        "gdn_norm_w": gain(ks[7], (n_a, GDN_DV)),
        "gdn_w_out": nrm(ks[8], (n_a, GDN_V_WIDTH, D_MODEL), GDN_V_WIDTH ** -0.5 * out_scale),
        "dil_w_in": nrm(ks[9], (n_b, D_MODEL, DIL_IN_WIDTH), D_MODEL ** -0.5),
        "dil_q_norm": gain(ks[10], (n_b, DIL_HEAD_DIM)),
        "dil_k_norm": gain(ks[11], (n_b, DIL_HEAD_DIM)),
        "dil_w_out": nrm(ks[12], (n_b, DIL_OUT_WIDTH, D_MODEL), DIL_OUT_WIDTH ** -0.5 * out_scale),
        "ffn_w_in": nrm(ks[13], (DEPTH, D_MODEL, 2 * FFN_HIDDEN), D_MODEL ** -0.5),
        "ffn_w_out": nrm(ks[14], (DEPTH, FFN_HIDDEN, D_MODEL), FFN_HIDDEN ** -0.5 * out_scale),
    }

def first_block(x, norm_mix, norm_ffn, gdn_w_in, gdn_conv_w, gdn_a_log, gdn_dt_bias, gdn_norm_w,
              gdn_w_out, dil_w_in, dil_q_norm, dil_k_norm, dil_w_out, ffn_w_in, ffn_w_out):
    for i in range(DEPTH):
        j = i // N_MIXERS
        hn = _rmsnorm(x, norm_mix[i])
        if i % N_MIXERS == 0:
            x = x + _gated_deltanet(hn, gdn_w_in[j], gdn_conv_w[j], gdn_a_log[j], gdn_dt_bias[j],
                                    gdn_norm_w[j], gdn_w_out[j])
        else:
            x = x + _dilated_attention(hn, dil_w_in[j], dil_q_norm[j], dil_k_norm[j], dil_w_out[j])
        x = x + _swiglu(_rmsnorm(x, norm_ffn[i]), ffn_w_in[i], ffn_w_out[i])
    return x


GRID_W = 64
CTX_LEN = 256
N_MLA = (DEPTH + 1) // 2
N_HYENA = DEPTH // 2

MLA_HEADS = 16
QK_NOPE = 64
QK_ROPE = 32
QK_DIM = QK_NOPE + QK_ROPE
V_HEAD = 64
Q_LORA = 512
KV_LORA = 256
ROPE_THETA = 10000.0
Q_BLOCK = 128

HY_BANDS = 16
HY_POS_DIM = 1 + 2 * HY_BANDS
HY_FILTER_HIDDEN = 64
HY_DECAY_SLOW = math.log(100.0) / 1.5
HY_DECAY_FAST = math.log(100.0) / 0.3
HY_FILTER_INIT = 0.02

D_FF = 2816

EPS = 1e-6
F32 = jnp.float32


def rmsnorm(x, g):
    xf = x.astype(F32)
    y = xf * lax.rsqrt(jnp.mean(xf * xf, axis=-1, keepdims=True) + EPS)
    return (y * g.astype(F32)).astype(x.dtype)

def modulate(h, shift, scale):
    return h * (1 + scale) + shift

def dwconv3(x, w, b):
    xp = jnp.pad(x, ((0, 0), (1, 1), (0, 0)))
    return xp[:, :-2] * w[0] + xp[:, 1:-1] * w[1] + xp[:, 2:] * w[2] + b

def axial_rope_tables(rows):
    row = jnp.repeat(jnp.arange(rows, dtype=F32), GRID_W)
    col = jnp.tile(jnp.arange(GRID_W, dtype=F32), rows)
    half = QK_ROPE // 2
    inv_freq = ROPE_THETA ** (-jnp.arange(0, half, 2, dtype=F32) / half)
    ang_r = row[:, None] * inv_freq
    ang_c = col[:, None] * inv_freq
    ang = jnp.concatenate([ang_r, ang_r, ang_c, ang_c], axis=-1)
    return jnp.cos(ang), jnp.sin(ang)

def apply_axial_rope(x, cos, sin):
    q = QK_ROPE // 4
    xf = x.astype(F32)
    rot = jnp.concatenate([-xf[..., q:2 * q], xf[..., :q], -xf[..., 3 * q:], xf[..., 2 * q:3 * q]], axis=-1)
    return (xf * cos + rot * sin).astype(x.dtype)

def mla_queries(h, w_dq, g_q, w_uq, cos, sin):
    B, L, _ = h.shape
    cq = rmsnorm(h @ w_dq, g_q)
    q = (cq @ w_uq).reshape(B, L, MLA_HEADS, QK_DIM)
    q_nope, q_pe = q[..., :QK_NOPE], q[..., QK_NOPE:]
    if cos is not None:
        q_pe = apply_axial_rope(q_pe, cos[None, :, None, :], sin[None, :, None, :])
    return jnp.concatenate([q_nope, q_pe], axis=-1)

def mla_keys_values(h, w_dkv, g_kv, w_uk, w_uv, cos, sin):
    B, L, _ = h.shape
    kv = h @ w_dkv
    ckv = rmsnorm(kv[..., :KV_LORA], g_kv)
    k_pe = kv[..., KV_LORA:]
    if cos is not None:
        k_pe = apply_axial_rope(k_pe, cos[None], sin[None])
    k_nope = (ckv @ w_uk).reshape(B, L, MLA_HEADS, QK_NOPE)
    v = (ckv @ w_uv).reshape(B, L, MLA_HEADS, V_HEAD)
    k_pe = jnp.broadcast_to(k_pe[:, :, None, :], (B, L, MLA_HEADS, QK_ROPE))
    return jnp.concatenate([k_nope, k_pe], axis=-1), v

def block_attention(q, k, v):
    B, Lq, H, dk = q.shape
    nblk = Lq // Q_BLOCK
    scale = 1.0 / math.sqrt(dk)
    qb = q.reshape(B, nblk, Q_BLOCK, H, dk).transpose(1, 0, 2, 3, 4)

    def one_block(qblk):
        s = jnp.einsum('bqhd,bkhd->bhqk', qblk, k).astype(F32) * scale
        p = jax.nn.softmax(s, axis=-1).astype(v.dtype)
        return jnp.einsum('bhqk,bkhd->bqhd', p, v)

    o = lax.map(one_block, qb)
    return o.transpose(1, 0, 2, 3, 4).reshape(B, Lq, H * v.shape[-1])

def hyena_pos_features(L):
    t = jnp.linspace(0.0, 1.0, L, dtype=F32)
    w = 2.0 * math.pi * jnp.arange(L, dtype=F32) / L
    f = jnp.linspace(1e-4, HY_BANDS - 1, HY_BANDS, dtype=F32)
    z = jnp.concatenate([t[:, None], jnp.cos(w[:, None] * f), -jnp.sin(w[:, None] * f)], axis=-1)
    return t, z

def hyena_filters(L, f_w1, f_b1, f_freq1, f_w2, f_b2, f_freq2, f_w3, decay):
    t, z = hyena_pos_features(L)
    h = jnp.sin(f_freq1.astype(F32) * (z @ f_w1.astype(F32) + f_b1.astype(F32)))
    h = jnp.sin(f_freq2.astype(F32) * (h @ f_w2.astype(F32) + f_b2.astype(F32)))
    h = h @ f_w3.astype(F32)
    window = jnp.exp(-t[:, None] * jnp.abs(decay.astype(F32))[None, :])
    d = h.shape[1] // 2
    return h[:, :d] * window, h[:, d:] * window

def two_sided_fftconv(u, h_fwd, h_bwd):
    L = u.shape[1]
    filt = jnp.concatenate([h_fwd, jnp.zeros((1, h_fwd.shape[1]), F32), h_bwd[1:][::-1]], axis=0)
    filt_f = jnp.fft.rfft(filt, n=2 * L, axis=0)
    u_f = jnp.fft.rfft(u.astype(F32), n=2 * L, axis=1)
    y = jnp.fft.irfft(u_f * filt_f[None], n=2 * L, axis=1)[:, :L]
    return y.astype(u.dtype)

def hyena_mixer(u, w_in, b_in, conv_w, conv_b, f_w1, f_b1, f_freq1, f_w2, f_b2, f_freq2, f_w3, decay, d_bias, w_out, b_out):
    L = u.shape[1]
    z = dwconv3(u @ w_in + b_in, conv_w, conv_b)
    x1, x2, v = jnp.split(z, 3, axis=-1)
    h_fwd, h_bwd = hyena_filters(L, f_w1, f_b1, f_freq1, f_w2, f_b2, f_freq2, f_w3, decay)
    v = v * x2
    y = (two_sided_fftconv(v, h_fwd, h_bwd) + v * d_bias) * x1
    return y @ w_out + b_out

def conv_ffn(h, w_up, conv_w, conv_b, w_down):
    z = dwconv3(h @ w_up, conv_w, conv_b)
    a, g = jnp.split(z, 2, axis=-1)
    return (jax.nn.silu(g) * a) @ w_down

def second_inputs(seed: int = 0) -> dict:
    key = jax.random.key(seed)
    ks = jax.random.split(key, 40)
    D = D_MODEL

    def nrm(i, shape, scale):
        return jax.random.normal(ks[i], shape, F32) * scale

    def gain(i, shape):
        return 1.0 + nrm(i, shape, 0.05)

    decay_base = jnp.linspace(HY_DECAY_SLOW, HY_DECAY_FAST, D, dtype=F32)
    return {
        'x': nrm(0, (BATCH, SEQ, D), 1.0),
        'c': nrm(1, (BATCH, D), 1.0),
        'ctx': nrm(2, (BATCH, CTX_LEN, D), 1.0),
        'c_ctx': nrm(3, (D,), 1.0),
        'mod_w': nrm(4, (DEPTH, D, 6 * D), D ** -0.5),
        'mod_b': nrm(5, (DEPTH, 6 * D), 0.02),
        'norm_mix_g': gain(6, (DEPTH, D)),
        'norm_ffn_g': gain(7, (DEPTH, D)),
        'mla_w_dq': nrm(8, (N_MLA, D, Q_LORA), D ** -0.5),
        'mla_g_q': gain(9, (N_MLA, Q_LORA)),
        'mla_w_uq': nrm(10, (N_MLA, Q_LORA, MLA_HEADS * QK_DIM), Q_LORA ** -0.5),
        'mla_w_dkv': nrm(11, (N_MLA, D, KV_LORA + QK_ROPE), D ** -0.5),
        'mla_g_kv': gain(12, (N_MLA, KV_LORA)),
        'mla_w_uk': nrm(13, (N_MLA, KV_LORA, MLA_HEADS * QK_NOPE), KV_LORA ** -0.5),
        'mla_w_uv': nrm(14, (N_MLA, KV_LORA, MLA_HEADS * V_HEAD), KV_LORA ** -0.5),
        'mla_w_o': nrm(15, (N_MLA, MLA_HEADS * V_HEAD, D), (MLA_HEADS * V_HEAD) ** -0.5),
        'hy_w_in': nrm(16, (N_HYENA, D, 3 * D), D ** -0.5),
        'hy_b_in': nrm(17, (N_HYENA, 3 * D), 0.02),
        'hy_conv_w': nrm(18, (N_HYENA, 3, 3 * D), 3 ** -0.5),
        'hy_conv_b': nrm(19, (N_HYENA, 3 * D), 0.02),
        'hy_f_w1': nrm(20, (N_HYENA, HY_POS_DIM, HY_FILTER_HIDDEN), HY_POS_DIM ** -0.5),
        'hy_f_b1': nrm(21, (N_HYENA, HY_FILTER_HIDDEN), 0.1),
        'hy_f_freq1': gain(22, (N_HYENA, HY_FILTER_HIDDEN)),
        'hy_f_w2': nrm(23, (N_HYENA, HY_FILTER_HIDDEN, HY_FILTER_HIDDEN), HY_FILTER_HIDDEN ** -0.5),
        'hy_f_b2': nrm(24, (N_HYENA, HY_FILTER_HIDDEN), 0.1),
        'hy_f_freq2': gain(25, (N_HYENA, HY_FILTER_HIDDEN)),
        'hy_f_w3': nrm(26, (N_HYENA, HY_FILTER_HIDDEN, 2 * D), HY_FILTER_INIT),
        'hy_decay': decay_base[None, :] * (1.0 + nrm(27, (N_HYENA, D), 0.05)),
        'hy_d_bias': nrm(28, (N_HYENA, D), 1.0),
        'hy_w_out': nrm(29, (N_HYENA, D, D), D ** -0.5),
        'hy_b_out': nrm(30, (N_HYENA, D), 0.02),
        'ffn_w_up': nrm(31, (DEPTH, D, 2 * D_FF), D ** -0.5),
        'ffn_conv_w': nrm(32, (DEPTH, 3, 2 * D_FF), 3 ** -0.5),
        'ffn_conv_b': nrm(33, (DEPTH, 2 * D_FF), 0.02),
        'ffn_w_down': nrm(34, (DEPTH, D_FF, D), D_FF ** -0.5),
        'final_g': gain(35, (D,)),
    }

def second_block(x, c, ctx, c_ctx, mod_w, mod_b, norm_mix_g, norm_ffn_g,
              mla_w_dq, mla_g_q, mla_w_uq, mla_w_dkv, mla_g_kv, mla_w_uk, mla_w_uv, mla_w_o,
              hy_w_in, hy_b_in, hy_conv_w, hy_conv_b, hy_f_w1, hy_f_b1, hy_f_freq1, hy_f_w2, hy_f_b2,
              hy_f_freq2, hy_f_w3, hy_decay, hy_d_bias, hy_w_out, hy_b_out,
              ffn_w_up, ffn_conv_w, ffn_conv_b, ffn_w_down, final_g):
    L = x.shape[1]
    ROWS = L // GRID_W
    cos, sin = axial_rope_tables(ROWS)
    silu_c = jax.nn.silu(c)
    silu_cc = jax.nn.silu(c_ctx)
    h_ctx = ctx
    for i in range(DEPTH):
        last = i == DEPTH - 1
        j = i // N_MIXERS
        mod_x = silu_c @ mod_w[i] + mod_b[i]
        mod_c = silu_cc @ mod_w[i] + mod_b[i]
        sh1, sc1, g1, sh2, sc2, g2 = [m[:, None, :] for m in jnp.split(mod_x, 6, axis=-1)]
        csh1, csc1, cg1, csh2, csc2, cg2 = jnp.split(mod_c, 6, axis=-1)
        hx = modulate(rmsnorm(x, norm_mix_g[i]), sh1, sc1)
        if i % N_MIXERS == 0:
            hc = modulate(rmsnorm(h_ctx, norm_mix_g[i]), csh1, csc1)
            qx = mla_queries(hx, mla_w_dq[j], mla_g_q[j], mla_w_uq[j], cos, sin)
            kx, vx = mla_keys_values(hx, mla_w_dkv[j], mla_g_kv[j], mla_w_uk[j], mla_w_uv[j], cos, sin)
            kc, vc = mla_keys_values(hc, mla_w_dkv[j], mla_g_kv[j], mla_w_uk[j], mla_w_uv[j], None, None)
            ox = block_attention(qx, jnp.concatenate([kc, kx], axis=1), jnp.concatenate([vc, vx], axis=1))
            x = x + g1 * (ox @ mla_w_o[j])
            if not last:
                qc = mla_queries(hc, mla_w_dq[j], mla_g_q[j], mla_w_uq[j], None, None)
                oc = block_attention(qc, kc, vc)
                h_ctx = h_ctx + cg1 * (oc @ mla_w_o[j])
        else:
            hy = (hy_w_in[j], hy_b_in[j], hy_conv_w[j], hy_conv_b[j], hy_f_w1[j], hy_f_b1[j], hy_f_freq1[j],
                  hy_f_w2[j], hy_f_b2[j], hy_f_freq2[j], hy_f_w3[j], hy_decay[j], hy_d_bias[j],
                  hy_w_out[j], hy_b_out[j])
            x = x + g1 * hyena_mixer(hx, *hy)
            if not last:
                hc = modulate(rmsnorm(h_ctx, norm_mix_g[i]), csh1, csc1)
                h_ctx = h_ctx + cg1 * hyena_mixer(hc, *hy)
        ffn = (ffn_w_up[i], ffn_conv_w[i], ffn_conv_b[i], ffn_w_down[i])
        x = x + g2 * conv_ffn(modulate(rmsnorm(x, norm_ffn_g[i]), sh2, sc2), *ffn)
        if not last:
            h_ctx = h_ctx + cg2 * conv_ffn(modulate(rmsnorm(h_ctx, norm_ffn_g[i]), csh2, csc2), *ffn)
    return rmsnorm(x, final_g)


def setup_inputs(seed=0):
    out = dict(first_inputs(seed))
    for name, value in second_inputs(seed + 1).items():
        if name != "x":
            out[name + "_2"] = value
    return out


def reference(
    x, norm_mix, norm_ffn, gdn_w_in, gdn_conv_w, gdn_a_log, gdn_dt_bias, gdn_norm_w, gdn_w_out,
    dil_w_in, dil_q_norm, dil_k_norm, dil_w_out, ffn_w_in, ffn_w_out, c_2, ctx_2, c_ctx_2,
    mod_w_2, mod_b_2, norm_mix_g_2, norm_ffn_g_2, mla_w_dq_2, mla_g_q_2, mla_w_uq_2,
    mla_w_dkv_2, mla_g_kv_2, mla_w_uk_2, mla_w_uv_2, mla_w_o_2, hy_w_in_2, hy_b_in_2,
    hy_conv_w_2, hy_conv_b_2, hy_f_w1_2, hy_f_b1_2, hy_f_freq1_2, hy_f_w2_2, hy_f_b2_2,
    hy_f_freq2_2, hy_f_w3_2, hy_decay_2, hy_d_bias_2, hy_w_out_2, hy_b_out_2, ffn_w_up_2,
    ffn_conv_w_2, ffn_conv_b_2, ffn_w_down_2, final_g_2,
):
    x = first_block(
        x, norm_mix, norm_ffn, gdn_w_in, gdn_conv_w, gdn_a_log, gdn_dt_bias, gdn_norm_w,
        gdn_w_out, dil_w_in, dil_q_norm, dil_k_norm, dil_w_out, ffn_w_in, ffn_w_out,
    )
    return second_block(
        x, c_2, ctx_2, c_ctx_2, mod_w_2, mod_b_2, norm_mix_g_2, norm_ffn_g_2, mla_w_dq_2,
        mla_g_q_2, mla_w_uq_2, mla_w_dkv_2, mla_g_kv_2, mla_w_uk_2, mla_w_uv_2, mla_w_o_2,
        hy_w_in_2, hy_b_in_2, hy_conv_w_2, hy_conv_b_2, hy_f_w1_2, hy_f_b1_2, hy_f_freq1_2,
        hy_f_w2_2, hy_f_b2_2, hy_f_freq2_2, hy_f_w3_2, hy_decay_2, hy_d_bias_2, hy_w_out_2,
        hy_b_out_2, ffn_w_up_2, ffn_conv_w_2, ffn_conv_b_2, ffn_w_down_2, final_g_2,
    )


_drawn_inputs = setup_inputs


def setup_inputs(seed=0):
    import zlib

    import numpy as np

    out = dict(_drawn_inputs(seed))
    spreads = {}
    factors = {'norm_mix': 3.857,
     'norm_ffn': 3.834,
     'gdn_norm_w': 6.998,
     'dil_q_norm': 8.0,
     'dil_k_norm': 8.0,
     'mla_g_q_2': 8.0,
     'mla_g_kv_2': 3.535,
     'hy_f_freq1_2': 3.749,
     'hy_f_freq2_2': 44.319,
     'hy_b_out_2': 157.681,
     'ffn_conv_b_2': 26.856,
     'norm_ffn_g_2': 8.0,
     'hy_b_in_2': 31.617,
     'hy_conv_b_2': 36.325,
     'hy_decay_2': 3.703}
    for name, (base, spread) in spreads.items():
        noise = np.random.default_rng([zlib.crc32(name.encode()), seed]).standard_normal(out[name].shape)
        drawn = base * np.exp(spread * noise) if base else spread * noise
        out[name] = jnp.asarray(drawn.astype(out[name].dtype))
    for name, factor in factors.items():
        out[name] = (out[name] * factor).astype(out[name].dtype)
    return out
```

```python
import concourse.bass as bass
from concourse import mybir
from concourse.alu_op_type import AluOpType as ALU
from contextlib import ExitStack
import numpy as np


F32 = mybir.dt.float32
F32R = mybir.dt.float32r
ACT = mybir.ActivationFunctionType
AX_X = mybir.AxisListType.X
P = 128
T = 512
D = 1024
KD = D // P
TB = T // P
EPS = 1e-6
FH = 2816
FT = FH // P
FTH = FT // 2
GH = 8
CTX = 256
KEYS = CTX + T
SLOTS, SLOT = 4, 4096


class Segment:

    def __init__(self, name, n, loads, slots=SLOTS, by_round=False, shift=0):
        self.name, self.n, self.slots, self.shift = name, n, slots, shift
        self.loads = loads if by_round else (lambda r, j: loads(r * slots + j))


class Stream:

    def __init__(self, ring, segments, landed, used):
        self.ring, self.segments, self.landed, self.used = ring, segments, landed, used
        self.start, self.previous, self.after, self.index = {}, [], [], {}
        n, last, count = 0, [None] * SLOTS, [0] * SLOTS
        self.segment_of = []
        for at, seg in enumerate(segments):
            self.start[seg.name] = n
            self.index[seg.name] = at
            seg.dmas = len(seg.loads(0, 0))
            for u in range(seg.n):
                s = (u + seg.shift) % seg.slots
                self.previous.append(last[s])
                last[s] = n
                count[s] += 16 * seg.dmas
                self.after.append(count[s])
                self.segment_of.append(at)
                n += 1
        self.total, self.issued = n, 0

    def slot(self, j):
        return self.ring[:, j, :]

    def load(self, sp, seg, r, j, previous):
        if previous is not None:
            sp.wait_ge(self.used, previous + 1)
        slot = (j + seg.shift) % seg.slots
        for dst, src in seg.loads(r, j):
            sp.dma_start(dst(self.slot(slot)), src).then_inc(self.landed[slot], 16)

    def prefetch(self, sp):
        while self.issued < self.total and self.previous[self.issued] is None:
            m = self.issued
            s = self.segments[self.segment_of[m]]
            v = m - self.start[s.name]
            self.load(sp, s, v // s.slots, v % s.slots, None)
            self.issued += 1

    def issue(self, sp, name):
        first, seg = self.start[name], self.segments[self.index[name]]
        u, n, q = self.issued - first, seg.n, seg.slots
        while u < min(q, n):
            self.load(sp, seg, u // q, u % q, self.previous[first + u])
            u += 1
        rounds = (n - u) // q
        if rounds >= 2:
            at = u
            with sp.Fori(0, rounds) as i:
                for j in range(q):
                    self.load(sp, seg, i + (at + j) // q, (at + j) % q, i * q + (at + j + first - q))
            u += rounds * q
        while u < n:
            self.load(sp, seg, u // q, u % q, self.previous[first + u])
            u += 1
        n_next = first + n
        self.issued = n_next
        while self.issued < min(n_next + SLOTS, self.total):
            m = self.issued
            if self.previous[m] is not None and self.previous[m] >= n_next:
                break
            s = self.segments[self.segment_of[m]]
            v = m - self.start[s.name]
            self.load(sp, s, v // s.slots, v % s.slots, self.previous[m])
            self.issued += 1

    def used_up(self, eng, name, u):
        eng.wait_ge(self.used, u + (self.start[name] + 1))

    def arrived(self, eng, name, i, j):
        seg, first = self.segments[self.index[name]], self.start[name]
        eng.wait_ge(self.landed[(j + seg.shift) % seg.slots], i * (16 * seg.dmas) + self.after[first + j])


def rounds(eng, n, body, step=SLOTS):
    full = n // step
    if full >= 2:
        with eng.Fori(0, full) as i:
            for j in range(step):
                body(i * step + j, i, j)
    elif full == 1:
        for j in range(step):
            body(j, 0, j)
    for j in range(n - full * step):
        body(full * step + j, full, j)


class Chain:

    def __init__(self, eng, sem):
        self.eng, self.sem, self.base, self.origin, self.k, self.per = eng, sem, 0, 0, 0, 0

    def unit(self, u, per):
        assert self.k == self.per, (self.k, self.per)
        self.origin, self.k, self.per = u * per + self.base, 0, per

    def begin(self):
        assert self.k == self.per
        self.origin, self.k, self.per = self.base, 0, 0

    def stop(self):
        self.base, self.k = self.base + self.k, 0

    def end(self, n):
        assert self.k == self.per, (self.k, self.per)
        self.base += n * self.per
        self.origin, self.k, self.per = self.base, 0, 0

    def __call__(self, ins):
        self.k += 1
        ins.then_inc(self.sem, 1)
        self.eng.wait_ge(self.sem, self.origin + self.k)


def bcast(ap, axis, n):
    v = ap.unsqueeze(axis)
    shape = list(v.shape)
    shape[axis] = n
    return v.to_broadcast(shape)


def network(nc, inp, const, out):
    with ExitStack() as ctx:
        def sb(name, shape):
            return ctx.enter_context(nc.sbuf_tensor(name, shape, F32))

        made = {}

        def sem(name):
            if name not in made:
                made[name] = nc.alloc_semaphore(name)
            return made[name]

        shared = ("norm_", "proj_")

        def retire(before):
            own = [name for name in made if name not in before and not name.startswith(shared)]
            nc.clear_and_free_semaphores([made.pop(name) for name in own])
            nc.all_engine_barrier()

        xT = sb("xT", [P, KD, T])
        hT = sb("hT", [P, KD, T])
        ring = sb("ring", [P, SLOTS, SLOT])
        ident = sb("ident", [P, P])
        ones = sb("ones", [P, P])
        csilu = sb("csilu", [P, KD, 2])
        rstd = sb("rstd", [P, 2, T])
        psum = ctx.enter_context(nc.psum_tensor("psum", [P, 8, 512], F32))
        bank = [psum[:, b, :] for b in range(8)]

        placed, rows = {}, 0
        vectors = [
            ("norm_mix", inp["norm_mix"].rearrange("l (k p) -> (l k) p", p=P)),
            ("norm_ffn", inp["norm_ffn"].rearrange("l (k p) -> (l k) p", p=P)),
            ("gdn_conv", inp["gdn_conv_w"].rearrange("a t (k p) -> (a t k) p", p=P)),
            ("gdn_norm", inp["gdn_norm_w"]),
            ("dil_q", inp["dil_q_norm"]),
            ("dil_k", inp["dil_k_norm"]),
            ("mix_g", inp["norm_mix_g_2"].rearrange("l (k p) -> (l k) p", p=P)),
            ("ffn_g", inp["norm_ffn_g_2"].rearrange("l (k p) -> (l k) p", p=P)),
            ("g_q", inp["mla_g_q_2"].rearrange("l (k p) -> (l k) p", p=P)),
            ("g_kv", inp["mla_g_kv_2"].rearrange("l (k p) -> (l k) p", p=P)),
            ("mod_b", inp["mod_b_2"].rearrange("l (k p) -> (l k) p", p=P)),
            ("c", inp["c_2"].rearrange("l (k p) -> (l k) p", p=P)),
            ("c_ctx", inp["c_ctx_2"].rearrange("(k p) -> k p", p=P)),
            ("hy_b_in", inp["hy_b_in_2"].rearrange("l (k p) -> (l k) p", p=P)),
            ("hy_conv_w", inp["hy_conv_w_2"].rearrange("a t (k p) -> (a t k) p", p=P)),
            ("hy_conv_b", inp["hy_conv_b_2"].rearrange("l (k p) -> (l k) p", p=P)),
            ("hy_d", inp["hy_d_bias_2"].rearrange("l (k p) -> (l k) p", p=P)),
            ("hy_b_out", inp["hy_b_out_2"].rearrange("l (k p) -> (l k) p", p=P)),
            ("f_b1", inp["hy_f_b1_2"]),
            ("f_freq1", inp["hy_f_freq1_2"]),
            ("f_b2", inp["hy_f_b2_2"]),
            ("f_freq2", inp["hy_f_freq2_2"]),
            ("ffn_conv_w", inp["ffn_conv_w_2"].rearrange("l t (k p) -> (l t k) p", p=P)),
            ("ffn_conv_b", inp["ffn_conv_b_2"].rearrange("l (k p) -> (l k) p", p=P)),
            ("final_g", inp["final_g_2"].rearrange("(k p) -> k p", p=P)),
        ]
        row_loads = []
        for name, ap in vectors:
            n, width = ap.shape
            placed[name] = rows
            at = 0
            while at < n:
                k = min(n - at, P - (rows + at) % P)
                for c in range(0, P, width):
                    row_loads.append(((rows + at) // P, (rows + at) % P, k, c, width, ap[at:at + k, :]))
                at += k
            rows += n
        groups = -(-rows // P)
        cols = sb("cols", [P, groups * P, 1])

        def col(name, i=0):
            return cols[:, placed[name] + i, :]

        def cols2(name, at, n):
            return cols[:, placed[name] + at:placed[name] + at + n, 0]

        modc = sb("modc", [P, 2, 48, 2])
        eps_col = sb("eps_col", [P, 1])
        gain = sb("gain", [P, 2 * KD, 1])
        arena_words = nc.sbuf_bytes_remaining // 4 - 64
        arena, arena_use, stages = None, [0], [0]
        owned = ctx.enter_context(ExitStack())

        def clear_arena(*split):
            owned.close()
            return fill_arena(owned, arena_words, *split)

        def fill_arena(stack, words, *split):
            nonlocal arena
            stages[0] += 1
            tensors = [stack.enter_context(nc.sbuf_tensor(f"{name}_{stages[0]}", shape, F32R)) for name, shape in split]
            left = words - sum(int(np.prod(shape[1:])) for _, shape in split)
            arena = stack.enter_context(nc.sbuf_tensor(f"arena_{stages[0]}", [P, left], F32))
            arena_use[0] = 0
            return tensors

        def take(*shape):
            n = int(np.prod(shape))
            a = arena_use[0]
            arena_use[0] += n
            assert arena_use[0] <= arena.shape[1], (arena_use, arena.shape)
            v = arena[:, a:a + n]
            if len(shape) == 2:
                return v.rearrange("p (a b) -> p a b", b=shape[1])
            if len(shape) == 3:
                return v.rearrange("p (a b c) -> p a b c", b=shape[1], c=shape[2])
            return v

        dve_chain = Chain(nc.vector, sem("dve_chain"))
        act_chain = Chain(nc.scalar, sem("act_chain"))
        pool_chain = Chain(nc.gpsimd, sem("pool_chain"))
        counted = {}

        def base(name, n):
            b = counted.get(name, 0)
            counted[name] = b + n
            return b

        def square_loads(w):
            g = w.rearrange("(k p) (u c) -> u p k c", p=P, c=4 * P)
            return lambda u: [(lambda s: s[:, 0:4096].rearrange("p (k c) -> p k c", k=KD), g[u])]

        def tile_loads(w, half):
            g = w.rearrange("(k p) (h u c) -> h u p k c", p=P, h=2, c=P)
            return lambda r, j: [(lambda s: s[:, 0:D].rearrange("p (k c) -> p k c", k=KD), g[j % 2, r * 2 + (j // 2 + half * FTH)])]

        def down_loads(w, half):
            g = w.rearrange("(h k p) (u c) -> h u p k c", h=2, p=P, c=P)[half]
            return lambda r, j: [(lambda s: s[:, 0:FTH * P].rearrange("p (k c) -> p k c", k=FTH), g[r * SLOTS + j])]

        segments = []

        def segment(name, n, loads, slots=SLOTS, by_round=False, shift=0):
            segments.append(Segment(name, n, loads, slots, by_round, shift))

        def stage_load():
            clear_arena()
            xtok = take(TB, D)
            vrows = take(groups, P)
            with nc.Block() as block:
                @block.sync
                def _(sp):
                    sp.dma_start(ident[:, :], const["ident"]).then_inc(sem("ident_in"), 16)
                    sp.dma_start(ones[:, :], const["ones"]).then_inc(sem("ident_in"), 16)
                    sp.dma_start(xtok, inp["x"].rearrange("b (c p) d -> p (b c) d", p=P)).then_inc(sem("x_in"), 16)
                    sp.wait_ge(sem("rows_clear"), 1)
                    for g, r, k, c, width, src in row_loads:
                        sp.dma_start(vrows[r:r + k, g, c:c + width], src).then_inc(sem("rows_in"), 16)
                    stream.prefetch(sp)

                @block.gpsimd
                def _(pool):
                    nc.gpsimd.memset(eps_col[:, :], EPS)
                    nc.gpsimd.memset(vrows, 0.0).then_inc(sem("rows_clear"), 1)

                @block.tensor
                def _(pe):
                    pe.wait_ge(sem("ident_in"), 32)
                    pe.wait_ge(sem("x_in"), 16)
                    for k in range(KD):
                        if k >= 4:
                            pe.wait_ge(sem("x_evac"), k - 3)
                        for c in range(TB):
                            m = nc.tensor.transpose(bank[k % 4][:, c * P:(c + 1) * P], xtok[:, c, k * P:(k + 1) * P], ident[:, :])
                        m.then_inc(sem("x_turned"), 1)
                    pe.wait_ge(sem("rows_in"), 16 * len(row_loads))
                    for g in range(groups):
                        m = nc.tensor.transpose(bank[4 + g // 4][:, g % 4 * P:(g % 4 + 1) * P], vrows[:, g, :], ident[:, :])
                        if g % 4 == 3 or g == groups - 1:
                            m.then_inc(sem("rows_turned"), 1)

                @block.vector
                def _(dve):
                    for k in range(KD):
                        dve.wait_ge(sem("x_turned"), k + 1)
                        nc.vector.tensor_copy(xT[:, k, :], bank[k % 4]).then_inc(sem("x_evac"), 1)
                    for b in range(-(-groups // 4)):
                        n = min(4, groups - 4 * b)
                        dve.wait_ge(sem("rows_turned"), b + 1)
                        nc.vector.tensor_copy(cols[:, 4 * b * P:(4 * b + n) * P, 0], bank[4 + b][:, 0:n * P]).then_inc(sem("cols_ready"), 1)

        class ResidualSums:
            def __init__(self, dst):
                self.dst, self.b = dst, 7
                self.s0, self.m0 = base("norm_squares", KD), base("norm_summed", 1)

            def square(self, act, k):
                nc.scalar.activation(self.dst[:, k, :], xT[:, k, :], ACT.Square).then_inc(sem("norm_squares"), 1)

            def sum(self, pe, k):
                pe.wait_ge(sem("norm_squares"), self.s0 + k + 1)
                m = nc.tensor.matmul(bank[self.b], ones[:, :], self.dst[:, k, :], start=(k == 0), stop=(k == KD - 1))
                if k == KD - 1:
                    m.then_inc(sem("norm_summed"), 1)

        ahead = []

        def sums_ahead(dst):
            ahead.append(ResidualSums(dst))
            return ahead[-1]

        class Norm:
            def __init__(self, src, dst, n, width, gains, shifts=None, tokens=T, b=7, r=0):
                self.src, self.dst, self.n, self.width = src, dst, n, width
                self.gains, self.shifts, self.tokens, self.b, self.r = gains, shifts, tokens, b, r
                self.squares, self.summed = sem("norm_squares"), sem("norm_summed")
                self.rooted, self.ready = sem("norm_rooted"), sem("norm_ready")
                self.sums = ahead.pop() if ahead and src is xT else None
                if self.sums:
                    self.m0 = self.sums.m0
                else:
                    self.s0, self.m0 = base("norm_squares", n), base("norm_summed", 1)
                self.q0 = base("norm_rooted", 1)
                self.r0 = base("norm_ready", n)
                if shifts is not None:
                    self.scaled, self.c0 = sem("norm_scaled"), base("norm_scaled", n)

            def act(self, act, after=None):
                for k in range(0 if self.sums else self.n):
                    nc.scalar.activation(self.dst[:, k, :], self.src[:, k, :], ACT.Square).then_inc(self.squares, 1)
                act.wait_ge(self.summed, self.m0 + 1)
                if after is not None:
                    after.wait(act)
                nc.scalar.activation(rstd[:, self.r, 0:self.tokens], bank[self.b][:, 0:self.tokens], ACT.Sqrt,
                                     bias=eps_col[:, :], scale=1.0 / self.width).then_inc(self.rooted, 1)
                if self.shifts is not None:
                    for k in range(self.n):
                        act.wait_ge(self.scaled, self.c0 + k + 1)
                        nc.scalar.activation(self.dst[:, k, :], self.dst[:, k, :], ACT.Identity, bias=self.shifts(k),
                                             scale=self.gains(k)).then_inc(self.ready, 1)

            def pe(self, pe):
                if self.sums:
                    return
                for k in range(self.n):
                    pe.wait_ge(self.squares, self.s0 + k + 1)
                    m = nc.tensor.matmul(bank[self.b][:, 0:self.tokens], ones[:, :], self.dst[:, k, :], start=(k == 0), stop=(k == self.n - 1))
                m.then_inc(self.summed, 1)

            def dve(self, dve):
                dve.wait_ge(self.rooted, self.q0 + 1)
                rs = rstd[:, self.r, 0:self.tokens]
                dve_chain(nc.vector.reciprocal(rs, rs))
                for k in range(self.n):
                    if self.shifts is None:
                        nc.vector.scalar_tensor_tensor(out=self.dst[:, k, :], in0=self.src[:, k, :], scalar=self.gains(k),
                                                       in1=rs, op0=ALU.mult, op1=ALU.mult).then_inc(self.ready, 1)
                    else:
                        nc.vector.tensor_tensor(self.dst[:, k, :], self.src[:, k, :], rs, ALU.mult).then_inc(self.scaled, 1)

            def wait(self, eng, k=None):
                eng.wait_ge(self.ready, self.r0 + (self.n if k is None else k + 1))

        def stage_store():
            clear_arena()
            ytok = take(TB, D)
            norm = Norm(xT, hT, KD, D, lambda k: col("final_g", k))
            with nc.Block() as block:
                @block.sync
                def _(sp):
                    for c in range(TB):
                        sp.wait_ge(sem("y_evac"), 2 * (c + 1))
                        sp.dma_start(out[0, c * P:(c + 1) * P, :], ytok[:, c, :]).then_inc(sem("y_out"), 16)
                    sp.wait_ge(sem("y_out"), 16 * TB)

                @block.tensor
                def _(pe):
                    norm.pe(pe)
                    norm.wait(pe)
                    for c in range(TB):
                        for g in range(2):
                            n = 2 * c + g
                            for k in range(4):
                                m = nc.tensor.transpose(bank[n][:, k * P:(k + 1) * P], hT[:, 4 * g + k, c * P:(c + 1) * P], ident[:, :])
                            m.then_inc(sem("y_turned"), 1)

                @block.scalar
                def _(act):
                    norm.act(act)

                @block.vector
                def _(dve):
                    dve_chain.begin()
                    norm.dve(dve)
                    dve_chain.stop()
                    for n in range(2 * TB):
                        dve.wait_ge(sem("y_turned"), n + 1)
                        nc.vector.tensor_copy(ytok[:, n // 2, n % 2 * 512:(n % 2 + 1) * 512], bank[n]).then_inc(sem("y_evac"), 1)

        def modulated(layer, kind, w, name, at):
            g = gain[:, w * KD:(w + 1) * KD, 0]

            def prepare():
                return nc.vector.scalar_tensor_tensor(out=g, in0=modc[:, layer, 24 * kind + KD:24 * kind + 2 * KD, w], scalar=1.0,
                                                      in1=cols2(name, at, KD), op0=ALU.add, op1=ALU.mult)
            return prepare, (lambda k: gain[:, w * KD + k, :]), (lambda k: modc[:, layer, 24 * kind + k, w:w + 1])

        def gate_of(layer, kind, u):
            return modc[:, layer, 24 * kind + 2 * KD + u, 0:1]

        class BackgroundModulation:
            WIDTH = 2 * D

            def __init__(self, layer, chunks):
                self.layer, self.chunks, self.ctx = layer, chunks, layer == 0
                self.sums = [ring[:, j, self.WIDTH:2 * self.WIDTH] for j in range(3)]
                self.ctx_sums = ring[:, 3, self.WIDTH:2 * self.WIDTH]
                self.l0 = [base(f"mod_landed{b}", 16 * 3 * KD // 2) for b in range(2)]
                self.u0 = base("mod_used", 3 * KD + 1) + 1
                self.z0, self.t0 = base("mod_cleared", 1), base("mod_columns", 1)

            def pool(self, pool, chunks_free):
                for j in range(4 if self.ctx else 3):
                    ins = nc.gpsimd.memset(ring[:, j, self.WIDTH:2 * self.WIDTH], 0.0)
                ins.then_inc(sem("mod_cleared"), 1)
                chunks_free(pool)
                w = inp["mod_w_2"][self.layer].rearrange("(k p) (b c) -> b k p c", p=P, b=3)
                for n in range(3 * KD):
                    if n >= 2:
                        pool.wait_ge(sem("mod_used"), self.u0 + n - 1)
                    pool.dma_start(self.chunks[:, n % 2, :], w[n // KD, n % KD]).then_inc(sem(f"mod_landed{n % 2}"), 16)

            def act(self, act):
                if self.layer == 0:
                    nc.scalar.activation(csilu[:, :, 0], cols2("c", 0, KD), ACT.Silu).then_inc(sem("c_ready"), 1)
                    nc.scalar.activation(csilu[:, :, 1], cols2("c_ctx", 0, KD), ACT.Silu).then_inc(sem("c_ready"), 1)

            def begin(self, dve):
                dve.wait_ge(sem("mod_cleared"), self.z0 + 1)
                dve.wait_ge(sem("c_ready"), 2)
                dve.sem_inc(sem("mod_used"), 1)

            def add(self, dve, b, i, j, step):
                k = i * step + j
                dve.wait_ge(sem(f"mod_landed{j % 2}"), i * (8 * step) + (self.l0[j % 2] + 64 * b + 16 * (j // 2 + 1)))
                dve.wait_ge(sem("mod_used"), k + (self.u0 + KD * b))
                c = self.chunks[:, j % 2, :]
                if self.ctx and b == 0:
                    nc.vector.scalar_tensor_tensor(out=self.ctx_sums, in0=c, scalar=csilu[:, k, 1:2],
                                                   in1=self.ctx_sums, op0=ALU.mult, op1=ALU.add)
                nc.vector.scalar_tensor_tensor(out=self.sums[b], in0=c, scalar=csilu[:, k, 0:1], in1=self.sums[b],
                                               op0=ALU.mult, op1=ALU.add).then_inc(sem("mod_used"), 1)

            def pe(self, pe):
                pe.wait_ge(sem("mod_used"), self.u0 + 3 * KD)
                for v in range(2 if self.ctx else 1):
                    for t in range(16 if v else 48):
                        sums = self.ctx_sums if v else self.sums[t // 16]
                        m = nc.tensor.matmul(bank[6][:, 96 * v + 2 * t:96 * v + 2 * t + 2], sums[:, t % 16 * P:(t % 16 + 1) * P], ones[:, 0:2], start=True, stop=True)
                m.then_inc(sem("mod_columns"), 1)

            def dve(self, dve):
                dve.wait_ge(sem("mod_columns"), self.t0 + 1)
                for v, n in ((0, 48), (1, 16))[0:2 if self.ctx else 1]:
                    nc.vector.tensor_tensor(modc[:, self.layer, 0:n, v], bank[6][:, 96 * v:96 * v + 2 * n].rearrange("p (t w) -> p t w", w=2)[:, :, 0],
                                            cols2("mod_b", 48 * self.layer, n), ALU.add)

        def stage_ffn(stage, layer, convolved=False):
            hH, hL, hidH, hidL, wH, wL = clear_arena(
                ("h_high", [P, KD, T]), ("h_low", [P, KD, T]), ("hid_high", [P, FTH, T]), ("hid_low", [P, FTH, T]),
                ("w_high", [P, 2, FTH * P]), ("w_low", [P, 2, FTH * P]))
            gated = hT[:, 0:2, :] if convolved else rstd
            value = hT[:, 2:4, :]
            mod = None
            if not convolved:
                mod = BackgroundModulation(layer, hT[:, :, :].rearrange("p (n k) t -> p n (k t)", n=2))
            if convolved:
                prepare, gains, shifts = modulated(layer, 1, 0, "ffn_g", layer * KD)
                norm = Norm(xT, hT, KD, D, gains, shifts)
            else:
                norm = Norm(xT, hT, KD, D, lambda k: col("norm_ffn", layer * KD + k))
            tail = sums_ahead(hT)
            ins = [f"ffn{stage}_in{half}" for half in range(2)]
            outs = [f"ffn{stage}_out{half}" for half in range(2)]
            U, V = 2 * FTH, FTH
            w0 = base("weight_high", 2 * (U + KD)), base("weight_low", 2 * (U + KD))
            h0 = base("h_rounded", KD), base("h_split", KD)
            g0 = base("gate_done", 2 * V if convolved else 0)
            s0 = base("silu_ready", 2 * V)
            f0 = base("pair_free", 2 * V + 2)
            r0 = base("hid_rounded", 2 * V)
            e0 = base("hid_split", 2 * V + 2)
            d0 = base("down_free", 2 * KD + 2)
            w_at = placed["ffn_conv_w"] + layer * 3 * 2 * FT
            b_at = placed["ffn_conv_b"] + layer * 2 * FT

            def number(half, down=0):
                return half * (U + KD) + down * U

            def round_weights(act, name, n0, i, u):
                words = D if name in ins else FTH * P
                stream.arrived(act, name, i + u // 4, u % 4)
                slot = (u + stream.segments[stream.index[name]].shift) % SLOTS
                nc.scalar.copy(wH[:, slot % 2, 0:words], ring[:, slot, 0:words]).then_inc(sem("weight_high"), 1)

            def split_weights(dve, name, n0, i, u):
                words = D if name in ins else FTH * P
                slot = (u + stream.segments[stream.index[name]].shift) % SLOTS
                dve.wait_ge(sem("weight_high"), i * 4 + (w0[0] + n0 + u + 1))
                nc.vector.tensor_tensor(wL[:, slot % 2, 0:words], ring[:, slot, 0:words], wH[:, slot % 2, 0:words].bitcast(F32),
                                        ALU.subtract).then_inc(sem("weight_low"), 1)

            def following(half, down, i, u):
                n = U if not down else KD
                if isinstance(i, int) and 4 * i + u + 2 >= n:
                    left = 4 * i + u + 2 - n
                    if down and half:
                        return None
                    return (ins[1], number(1), 0, left) if down else (outs[half], number(half, 1), 0, left)
                return (outs if down else ins)[half], number(half, down), i, u + 2

            def step(eng, half, down, i, u, split):
                stream.used_up(eng, (outs if down else ins)[half], i * 4 + u)
                nxt = following(half, down, i, u)
                if nxt is not None:
                    split(eng, *nxt)

            def pairs(eng, body, last):
                body(0, 0)
                n = (V - 1 - last) // 2
                with eng.Fori(0, n) as i:
                    for p in (1, 2):
                        body(i, p)
                for p in range(last):
                    body(0, 2 * n + 1 + p)

            def passes(b, w, k, x_high, x_low, n):
                a, z = wH[:, w, k * P:(k + 1) * P], wL[:, w, k * P:(k + 1) * P]
                nc.tensor.matmul(b, a, x_high[:, k, :], start=(k == 0), stop=False)
                nc.tensor.matmul(b, a, x_low[:, k, :], start=False, stop=False)
                return nc.tensor.matmul(b, z, x_high[:, k, :], start=False, stop=(k == n - 1))

            def hidden(t, i, p):
                return t[:, i * 2 + p, :]

            with nc.Block() as block:
                @block.sync
                def _(sp):
                    for half in range(2):
                        stream.issue(sp, ins[half])
                        stream.issue(sp, outs[half])

                if mod is not None:
                    @block.gpsimd
                    def _(pool):
                        mod.pool(pool, lambda eng: eng.wait_ge(sem("h_split"), h0[1] + KD))

                @block.tensor
                def _(pe):
                    pe.sem_inc(sem("pair_free"), 2)
                    pe.sem_inc(sem("hid_split"), 2)
                    pe.sem_inc(sem("down_free"), 2)
                    norm.pe(pe)

                    def up(half, first):
                        def pair(i, p):
                            pe.wait_ge(sem("pair_free"), i * 2 + (f0 + half * V + p + 1))
                            for h in range(2):
                                u = 2 * p + h
                                pe.wait_ge(sem("weight_low"), i * 4 + (w0[1] + number(half) + u + 1))
                                for k in range(KD):
                                    if first and isinstance(i, int) and u == 0:
                                        pe.wait_ge(sem("h_split"), h0[1] + k + 1)
                                    m = passes(bank[p % 2 * 2 + h], u % 2, k, hH, hL, KD)
                                m.then_inc(sem("unit_done"), 1)
                        pairs(pe, pair, 0)

                    def down(half):
                        pe.wait_ge(sem("hid_split"), e0 + 2 + half * V + V - 1)

                        def unit(u, i, j):
                            pe.wait_ge(sem("down_free"), u + (d0 + half * KD + 1))
                            pe.wait_ge(sem("weight_low"), u + (w0[1] + number(half, 1) + 1))
                            for k in range(FTH):
                                if k == FTH - 1:
                                    pe.wait_ge(sem("hid_split"), e0 + 2 + half * V + V)
                                m = passes(bank[4 + j % 2], j % 2, k, hidH, hidL, FTH)
                            m.then_inc(sem("unit_done"), 1)
                            if half and u:
                                tail.sum(pe, u - 1)
                        if half:
                            for u in range(KD):
                                unit(u, 0, u)
                            tail.sum(pe, KD - 1)
                        else:
                            rounds(pe, KD, unit)
                    up(0, True)
                    down(0)
                    up(1, False)
                    if mod is not None:
                        mod.pe(pe)
                    down(1)

                @block.scalar
                def _(act):
                    if mod is not None:
                        mod.act(act)
                    for u in range(2):
                        round_weights(act, ins[0], 0, 0, u)
                    norm.act(act)
                    for k in range(KD):
                        norm.wait(act, k)
                        nc.scalar.copy(hH[:, k, :], hT[:, k, :]).then_inc(sem("h_rounded"), 1)
                    if not convolved:
                        act.wait_ge(sem("h_split"), h0[1] + KD)

                    def up(half):
                        def pair(i, p):
                            step(act, half, 0, i, 2 * p, round_weights)
                            g = gated[:, p % 2, :]
                            if not convolved:
                                act.wait_ge(sem("hid_split"), i * 2 + (e0 + half * V + p + 1))
                                nc.scalar.activation(g, bank[p % 2 * 2], ACT.Silu).then_inc(sem("silu_ready"), 1)
                            step(act, half, 0, i, 2 * p + 1, round_weights)
                            if convolved:
                                act.wait_ge(sem("gate_done"), i * 2 + (g0 + half * V + p + 1))
                                nc.scalar.activation(g, g, ACT.Silu).then_inc(sem("silu_ready"), 1)
                            act.wait_ge(sem("pair_free"), i * 2 + (f0 + 2 + half * V + p + 1))
                            nc.scalar.copy(hidden(hidH, i, p), g).then_inc(sem("hid_rounded"), 1)
                        pairs(act, pair, 2)
                    for half in range(2):
                        up(half)
                        for u in range(KD):
                            step(act, half, 1, 0, u, round_weights)
                            if half:
                                act.wait_ge(sem("down_free"), d0 + 2 + KD + u + 1)
                                tail.square(act, u)

                @block.vector
                def _(dve):
                    dve_chain.begin()
                    for u in range(2):
                        split_weights(dve, ins[0], 0, 0, u)
                    if convolved:
                        dve_chain(prepare())
                    norm.dve(dve)
                    dve_chain.stop()
                    for k in range(KD):
                        dve.wait_ge(sem("h_rounded"), h0[0] + k + 1)
                        nc.vector.tensor_tensor(hL[:, k, :], hT[:, k, :], hH[:, k, :].bitcast(F32), ALU.subtract).then_inc(sem("h_split"), 1)
                    if mod is not None:
                        mod.begin(dve)

                    def convolve(z, b, tile):
                        dve_chain(nc.vector.tensor_scalar(z, b, cols[:, tile + (w_at + 2 * FT), :], cols[:, tile + b_at, :], ALU.mult, ALU.add))
                        dve_chain(nc.vector.scalar_tensor_tensor(out=z[:, 1:T], in0=b[:, 0:T - 1], scalar=cols[:, tile + w_at, :],
                                                                 in1=z[:, 1:T], op0=ALU.mult, op1=ALU.add))
                        return nc.vector.scalar_tensor_tensor(out=z[:, 0:T - 1], in0=b[:, 1:T], scalar=cols[:, tile + (w_at + 4 * FT), :],
                                                              in1=z[:, 0:T - 1], op0=ALU.mult, op1=ALU.add)

                    def up(half):
                        def pair(i, p):
                            g, b = gated[:, p % 2, :], bank[p % 2 * 2 + 1]
                            if convolved:
                                dve_chain.unit(i * 2 + p, 5)
                            step(dve, half, 0, i, 2 * p, split_weights)
                            if convolved:
                                dve_chain(convolve(value[:, p % 2, :], bank[p % 2 * 2], i * 2 + (half * V + p)))
                            elif mod is not None and not isinstance(i, int):
                                mod.add(dve, 2 * half, i, p - 1, 2)
                            step(dve, half, 0, i, 2 * p + 1, split_weights)
                            if convolved:
                                convolve(g, b, i * 2 + (FT + half * V + p)).then_inc(sem("gate_done"), 1)
                                b = value[:, p % 2, :]
                            dve.wait_ge(sem("silu_ready"), i * 2 + (s0 + half * V + p + 1))
                            nc.vector.tensor_tensor(g, g, b, ALU.mult).then_inc(sem("pair_free"), 1)
                            dve.wait_ge(sem("hid_rounded"), i * 2 + (r0 + half * V + p + 1))
                            nc.vector.tensor_tensor(hidden(hidL, i, p), g, hidden(hidH, i, p).bitcast(F32), ALU.subtract).then_inc(sem("hid_split"), 1)
                        pairs(dve, pair, 2)
                        if convolved:
                            dve_chain.end(V)
                    for half in range(2):
                        up(half)
                        for u in range(KD):
                            step(dve, half, 1, 0, u, split_weights)
                            if convolved:
                                added = nc.vector.scalar_tensor_tensor(out=xT[:, u, :], in0=bank[4 + u % 2], scalar=gate_of(layer, 1, u), in1=xT[:, u, :],
                                                                      op0=ALU.mult, op1=ALU.add)
                            else:
                                added = nc.vector.tensor_tensor(xT[:, u, :], xT[:, u, :], bank[4 + u % 2], ALU.add)
                            added.then_inc(sem("down_free"), 1)
                            if mod is not None and half == 0:
                                mod.add(dve, 1, 0, u, KD)
                    if mod is not None:
                        mod.dve(dve)


        HEADS, NOPE, ROPE, QK, VH = 16, 64, 32, 96, 64
        QL, KVL = 4, 2
        KB = KEYS // P

        def stage_mla():
            clear_arena()
            vtok = take(KB, HEADS * VH)
            otok = take(TB, HEADS * VH)
            oT = hT
            cqT = take(QL, T)
            ckvT = take(KVL, KEYS)
            kT = take(2, KEYS)
            qT = take(2, T)
            cos, sin = take(T), take(T)
            roped = take(T)
            rot = take(P)
            mark = arena_use[0]
            hcT = take(KD, CTX)
            ctxT = take(KD, CTX)
            ctok = otok.rearrange("p a b -> p (a b)")[:, 0:2 * D].rearrange("p (a b) -> p a b", b=D)
            lat = take(KVL, KEYS)
            latq = vtok.rearrange("p a b -> p (a b)")[:, 0:QL * T].rearrange("p (a b) -> p a b", b=T)

            prep_x, gx, shx = modulated(0, 0, 0, "mix_g", 0)
            prep_c, gc, shc = modulated(0, 0, 1, "mix_g", 0)
            norm_x = Norm(xT, hT, KD, D, gx, shx)
            norm_c = Norm(ctxT, hcT, KD, D, gc, shc, tokens=CTX, b=6, r=1)
            norm_q = Norm(latq, cqT, QL, QL * P, lambda k: col("g_q", k))
            norm_k1 = Norm(lat[:, :, 0:T], ckvT[:, :, 0:T], KVL, KVL * P, lambda k: col("g_kv", k), b=6)
            norm_k2 = Norm(lat[:, :, T:KEYS], ckvT[:, :, T:KEYS], KVL, KVL * P, lambda k: col("g_kv", k), tokens=KEYS - T, b=5, r=1)
            with nc.Block() as block:
                @block.sync
                def _(sp):
                    sp.dma_start(ctok, inp["ctx_2"].rearrange("b (c p) d -> p (b c) d", p=P)).then_inc(sem("ctx_in"), 16)
                    sp.dma_start(cos, const["rope_cos"]).then_inc(sem("rope_in"), 16)
                    sp.dma_start(sin, const["rope_sin"]).then_inc(sem("rope_in"), 16)
                    sp.dma_start(rot, const["rope_rot"]).then_inc(sem("rope_in"), 16)
                    stream.issue(sp, "mla_dq")
                    stream.issue(sp, "mla_dkv")
                    stream.issue(sp, "mla_uv")

                @block.tensor
                def _(pe):
                    pe.wait_ge(sem("ctx_in"), 16)
                    for k in range(KD):
                        for c in range(2):
                            m = nc.tensor.transpose(bank[k // 2][:, (k % 2 * 2 + c) * P:(k % 2 * 2 + c + 1) * P], ctok[:, c, k * P:(k + 1) * P], ident[:, :])
                        if k % 2:
                            m.then_inc(sem("ctx_turned"), 1)
                    norm_x.pe(pe)
                    norm_c.pe(pe)
                    norm_x.wait(pe)
                    pe.wait_ge(sem("ctx_evac"), 4)
                    stream.arrived(pe, "mla_dq", 0, 0)
                    w = stream.slot(0).rearrange("p (k c) -> p k c", k=KD)
                    for t in range(QL):
                        for k in range(KD):
                            m = nc.tensor.matmul(bank[t], w[:, k, t * P:(t + 1) * P], hT[:, k, :], start=(k == 0), stop=(k == KD - 1))
                        if t < QL - 1:
                            m.then_inc(sem("latq_ready"), 1)
                    m.then_inc(sem("unit_done"), 1)
                    norm_c.wait(pe)
                    stream.arrived(pe, "mla_dkv", 0, 0)
                    w = stream.slot(0)[:, 0:KD * 288].rearrange("p (k c) -> p k c", k=KD)
                    pe.wait_ge(sem("lat_evac"), QL)
                    for part, (src, n) in enumerate(((hcT, CTX), (hT, T))):
                        for t in range(KVL):
                            for k in range(KD):
                                m = nc.tensor.matmul(bank[2 * part + t][:, 0:n], w[:, k, t * P:(t + 1) * P], src[:, k, :], start=(k == 0), stop=(k == KD - 1))
                            m.then_inc(sem("latk_ready"), 1)
                    for part, (src, n) in enumerate(((hcT, CTX), (hT, T))):
                        for k in range(KD):
                            m = nc.tensor.matmul(bank[4 + 3 * part][NOPE:QK, 0:n], w[:, k, 2 * P:2 * P + ROPE], src[:, k, :], start=(k == 0), stop=(k == KD - 1))
                        if part == 0:
                            m.then_inc(sem("kpe_ready"), 1)
                    m.then_inc(sem("unit_done"), 1)
                    norm_q.b = 5
                    norm_q.pe(pe)
                    pe.wait_ge(sem("rope_in"), 48)
                    pe.wait_ge(sem("kpe_raw"), 1)
                    nc.tensor.matmul(bank[7][NOPE:QK, :], rot[NOPE:QK, 0:ROPE], roped[NOPE:QK, :], start=True, stop=True).then_inc(sem("kpe_rot"), 1)
                    norm_k1.pe(pe)
                    norm_q.wait(pe)
                    norm_k2.pe(pe)
                    norm_k1.wait(pe)
                    norm_k2.wait(pe)
                    stream.arrived(pe, "mla_uv", 0, 0)
                    w = stream.slot(0)[:, 0:KVL * D].rearrange("p (k c) -> p k c", k=KVL)
                    for c in range(KB):
                        for h in range(2):
                            n = 2 * c + h
                            if n >= 4:
                                pe.wait_ge(sem("v_evac"), n - 3)
                            for k in range(KVL):
                                m = nc.tensor.matmul(bank[n % 4], ckvT[:, k, c * P:(c + 1) * P], w[:, k, h * 512:(h + 1) * 512], start=(k == 0), stop=(k == KVL - 1))
                            m.then_inc(sem("v_ready" if n < 2 * KB - 1 else "unit_done"), 1)

                @block.scalar
                def _(act):
                    for b in range(4):
                        act.wait_ge(sem("ctx_turned"), b + 1)
                        ins = nc.scalar.copy(ctxT[:, 2 * b:2 * b + 2, :], bank[b].rearrange("p (a b) -> p a b", a=2))
                        ins.then_inc(sem("ctx_evac"), 1)
                    act.wait_ge(sem("ctx_evac"), 4)
                    norm_x.act(act)
                    norm_c.act(act)
                    for t in range(QL):
                        if t < QL - 1:
                            act.wait_ge(sem("latq_ready"), t + 1)
                        else:
                            stream.used_up(act, "mla_dq", 0)
                        nc.scalar.copy(latq[:, t, :], bank[t]).then_inc(sem("lat_evac"), 1)
                    for n, (b, t, a, m) in enumerate(((0, 0, 0, CTX), (1, 1, 0, CTX), (2, 0, CTX, T), (3, 1, CTX, T))):
                        act.wait_ge(sem("latk_ready"), n + 1)
                        nc.scalar.copy(lat[:, t, a:a + m], bank[b][:, 0:m]).then_inc(sem("lat_evac"), 1)
                    act.wait_ge(sem("kpe_ready"), 1)
                    for b in range(2):
                        nc.scalar.copy(kT[NOPE:QK, b, 0:CTX], bank[4][NOPE:QK, 0:CTX]).then_inc(sem("kpe_ctx"), 1)
                    stream.used_up(act, "mla_dkv", 0)
                    nc.scalar.copy(roped[NOPE:QK, :], bank[7][NOPE:QK, :]).then_inc(sem("kpe_raw"), 1)
                    act.wait_ge(sem("lat_evac"), 8)
                    norm_q.act(act, norm_c)
                    norm_k1.act(act, norm_q)
                    norm_k2.act(act, norm_k1)

                @block.vector
                def _(dve):
                    dve.wait_ge(sem("ctx_evac"), 4)
                    dve_chain.begin()
                    dve_chain(prep_x())
                    dve_chain(prep_c())
                    norm_x.dve(dve)
                    norm_c.dve(dve)
                    norm_q.dve(dve)
                    dve.wait_ge(sem("rope_in"), 48)
                    dve.wait_ge(sem("kpe_rot"), 1)
                    turned = rstd[NOPE:QK, 1, :]
                    dve_chain(nc.vector.tensor_tensor(turned, sin[NOPE:QK, :], bank[7][NOPE:QK, :], ALU.mult))
                    dve_chain(nc.vector.tensor_tensor(roped[NOPE:QK, :], roped[NOPE:QK, :], cos[NOPE:QK, :], ALU.mult))
                    for b in range(2):
                        dve_chain(nc.vector.tensor_tensor(kT[NOPE:QK, b, CTX:KEYS], roped[NOPE:QK, :], turned, ALU.add))
                    norm_k1.dve(dve)
                    norm_k2.dve(dve)
                    dve_chain.stop()
                    for n in range(2 * KB):
                        if n < 2 * KB - 1:
                            dve.wait_ge(sem("v_ready"), n + 1)
                        else:
                            stream.used_up(dve, "mla_uv", 0)
                        nc.vector.tensor_copy(vtok[:, n // 2, n % 2 * 512:(n % 2 + 1) * 512], bank[n % 4]).then_inc(sem("v_evac"), 1)

            arena_use[0] = mark
            probs = take(2, KEYS)
            probsT = take(2, KEYS)
            lsum = take(2, 4)
            SCALE = float(1.0 / np.sqrt(QK))
            BQ, BX, BT, BO = 0, 7, 4, 6

            def flat(b, n):
                return psum[:, b:b + 2, :].rearrange("p a b -> p (a b)")[:, 0:n]

            def walk(eng, unit):
                with eng.Fori(0, 3) as i:
                    for j in range(2):
                        unit(i * 2 + j, i, j, False)
                for j in range(2):
                    unit(6 + j, 3, j, j == 1)

            vheads = vtok.rearrange("p c (h d) -> p h c d", d=VH)
            oheads = otok.rearrange("p c (h d) -> p h c d", d=VH)
            with nc.Block() as block:
                @block.sync
                def _(sp):
                    stream.issue(sp, "mla_heads")

                @block.tensor
                def _(pe):
                    pe.sem_inc(sem("o_free"), 1)

                    def queries(p, slot, g):
                        w = stream.slot(slot)[:, 0:768].rearrange("p (k c) -> p k c", k=QL)
                        for k in range(QL):
                            m = nc.tensor.matmul(bank[BX][0:QK, :], w[:, k, p * QK:(p + 1) * QK], cqT[:, k, :], start=(k == 0), stop=(k == QL - 1))
                        m.then_inc(sem("q_made"), 1)

                    def rotation_and_keys(p, slot, g):
                        pe.wait_ge(sem("q_raw"), g + 1)
                        w = stream.slot(slot)[:, 768:1024].rearrange("p (k c) -> p k c", k=KVL)
                        for k in range(KVL):
                            m = nc.tensor.matmul(bank[BX][0:NOPE, :], w[:, k, p * NOPE:(p + 1) * NOPE], ckvT[:, k, 0:T], start=(k == 0), stop=(k == KVL - 1))
                        m.then_inc(sem("k_made"), 1)
                        nc.tensor.matmul(bank[BX][NOPE:QK, :], rot[NOPE:QK, 0:ROPE], qT[NOPE:QK, p, :], start=True, stop=True).then_inc(sem("q_turned"), 1)

                    def more_keys(p, slot, g):
                        pe.wait_ge(sem("k_ready"), g * 2 + 1)
                        pe.wait_ge(sem("q_roped"), g + 1)
                        w = stream.slot(slot)[:, 768:1024].rearrange("p (k c) -> p k c", k=KVL)
                        for k in range(KVL):
                            m = nc.tensor.matmul(bank[BX][0:NOPE, 0:KEYS - T], w[:, k, p * NOPE:(p + 1) * NOPE], ckvT[:, k, T:KEYS], start=(k == 0), stop=(k == KVL - 1))
                        m.then_inc(sem("unit_done" if p else "k2_made"), 1)

                    def scores(g, p, qt):
                        if qt == 0:
                            pe.wait_ge(sem("k_ready"), g * 2 + 2)
                            pe.wait_ge(sem("q_roped"), g + 1)
                        b = qt % 2 * 2
                        q = qT[0:QK, p, qt * P:(qt + 1) * P]
                        nc.tensor.matmul(bank[b], q, kT[0:QK, p, 0:T], start=True, stop=True)
                        nc.tensor.matmul(bank[b + 1][:, 0:KEYS - T], q, kT[0:QK, p, T:KEYS], start=True, stop=True).then_inc(sem("scores_ready"), 1)

                    stream.arrived(pe, "mla_heads", 0, 0)
                    queries(0, 0, 0)
                    rotation_and_keys(0, 0, 0)
                    more_keys(0, 0, 0)
                    scores(0, 0, 0)

                    def unit(u, i, j, last):
                        for p in range(2):
                            g = u * 2 + p
                            nslot, np_ = (j, 1) if p == 0 else ((j + 1) % 2, 0)
                            more = not (last and p == 1)
                            for qt in range(TB):
                                n = u * 8 + (4 * p + qt)
                                if qt < TB - 1:
                                    scores(g, p, qt + 1)
                                elif more:
                                    scores(g + 1, np_, 0)
                                pe.wait_ge(sem("probs_ready"), n + 1)
                                for c in range(KB):
                                    m = nc.tensor.transpose(bank[BT + c // 4][:, c % 4 * P:(c % 4 + 1) * P], probs[:, qt % 2, c * P:(c + 1) * P], ident[:, :])
                                m.then_inc(sem("probs_turned"), 1)
                                if more and qt == 0:
                                    if p == 1:
                                        stream.arrived(pe, "mla_heads", i + (j + 1) // 2, (j + 1) % 2)
                                    pe.wait_ge(sem("k_ready"), g * 2 + 2)
                                    queries(np_, nslot, g + 1)
                                elif more and qt == 1:
                                    rotation_and_keys(np_, nslot, g + 1)
                                elif more and qt == 2:
                                    more_keys(np_, nslot, g + 1)
                                pe.wait_ge(sem("probsT_low"), n + 1)
                                pe.wait_ge(sem("probsT_high"), n + 1)
                                pe.wait_ge(sem("o_free"), n + 1)
                                for c in range(KB):
                                    m = nc.tensor.matmul(bank[BO][:, 0:VH], probsT[:, qt % 2, c * P:(c + 1) * P], vheads[:, g, c, :], start=(c == 0), stop=(c == KB - 1))
                                m.then_inc(sem("o_ready"), 1)
                    walk(pe, unit)

                @block.scalar
                def _(act):
                    def raw(p, g):
                        act.wait_ge(sem("q_made"), g + 1)
                        nc.scalar.copy(qT[0:QK, p, :], bank[BX][0:QK, :]).then_inc(sem("q_raw"), 1)

                    def keys(p, g):
                        act.wait_ge(sem("k_made"), g + 1)
                        nc.scalar.copy(kT[0:NOPE, p, 0:T], bank[BX][0:NOPE, :]).then_inc(sem("k_ready"), 1)

                    def more_keys(p, u):
                        if p:
                            stream.used_up(act, "mla_heads", u)
                        else:
                            act.wait_ge(sem("k2_made"), u + 1)
                        nc.scalar.copy(kT[0:NOPE, p, T:KEYS], bank[BX][0:NOPE, 0:KEYS - T]).then_inc(sem("k_ready"), 1)

                    def softmax(n, b):
                        act.wait_ge(sem("max_ready"), n + 1)
                        nc.scalar.activation(probs[:, b, :], flat(2 * b, KEYS), ACT.Exp, bias=lsum[:, b, 0:1], scale=SCALE,
                                             accum_out=lsum[:, b, 1:2]).then_inc(sem("probs_ready"), 1)

                    raw(0, 0)
                    keys(0, 0)
                    more_keys(0, 0)
                    softmax(0, 0)

                    def unit(u, i, j, last):
                        for p in range(2):
                            more = not (last and p == 1)
                            for qt in range(TB):
                                n = u * 8 + (4 * p + qt)
                                act.wait_ge(sem("probs_turned"), n + 1)
                                nc.scalar.copy(probsT[:, qt % 2, T:KEYS], bank[BT + 1][:, 0:KEYS - T]).then_inc(sem("probsT_high"), 1)
                                if more or qt < TB - 1:
                                    softmax(n + 1, (qt + 1) % 2)
                                if more and qt == 0:
                                    raw(1 - p, u * 2 + (p + 1))
                                elif more and qt == 1:
                                    keys(1 - p, u * 2 + (p + 1))
                                elif more and qt == 2:
                                    more_keys(1 - p, u + p)
                    walk(act, unit)

                @block.vector
                def _(dve):
                    def rope(p, g):
                        dve.wait_ge(sem("q_turned"), g + 1)
                        q, r = qT[NOPE:QK, p, :], roped[NOPE:QK, :]
                        dve_chain(nc.vector.tensor_tensor(r, sin[NOPE:QK, :], bank[BX][NOPE:QK, :], ALU.mult))
                        dve_chain(nc.vector.tensor_tensor(q, q, cos[NOPE:QK, :], ALU.mult))
                        nc.vector.tensor_tensor(q, q, r, ALU.add).then_inc(sem("q_roped"), 1)

                    def maximum(n, b):
                        dve.wait_ge(sem("scores_ready"), n + 1)
                        dve_chain(nc.vector.reduce_max(lsum[:, b, 0:1], flat(2 * b, KEYS), AX_X))
                        nc.vector.tensor_scalar(lsum[:, b, 0:1], lsum[:, b, 0:1], -SCALE, None, ALU.mult).then_inc(sem("max_ready"), 1)

                    dve_chain.begin()
                    rope(0, 0)
                    maximum(0, 0)
                    dve_chain.stop()

                    def unit(u, i, j, last):
                        if not isinstance(u, int):
                            dve_chain.unit(u, 8 * 2 + 2 * 2)
                        for p in range(2):
                            more = not (last and p == 1)
                            for qt in range(TB):
                                n = u * 8 + (4 * p + qt)
                                if more or qt < TB - 1:
                                    maximum(n + 1, (qt + 1) % 2)
                                dve.wait_ge(sem("probs_turned"), n + 1)
                                nc.vector.tensor_copy(probsT[:, qt % 2, 0:T], bank[BT]).then_inc(sem("probsT_low"), 1)
                                dve.wait_ge(sem("probs_ready"), n + 1)
                                dve_chain(nc.vector.reciprocal(lsum[:, qt % 2, 2:3], lsum[:, qt % 2, 1:2]))
                                dve.wait_ge(sem("o_ready"), n + 1)
                                nc.vector.tensor_scalar(oheads[:, u * 2 + p, qt, :], bank[BO][:, 0:VH], lsum[:, qt % 2, 2:3], None, ALU.mult).then_inc(sem("o_free"), 1)
                                if more and qt == 1:
                                    rope(1 - p, u * 2 + (p + 1))
                    with dve.Fori(0, 3) as i:
                        for j in range(2):
                            unit(i * 2 + j, i, j, False)
                    dve_chain.end(6)
                    dve_chain.begin()
                    for j in range(2):
                        unit(6 + j, 3, j, j == 1)
                    dve_chain.stop()

            project(otok, oT, "mla_o", lambda u: gate_of(0, 0, u), sums_ahead(otok.rearrange("p c (a t) -> p (c a) t", t=T)))

        def project(otok, oT, seg, gate, tail):
            o0, e0 = base("o_turned", 8), base("oT_evac", 8)
            with nc.Block() as block:
                @block.sync
                def _(sp):
                    stream.issue(sp, seg)

                @block.tensor
                def _(pe):
                    for k in range(KD):
                        for c in range(TB):
                            m = nc.tensor.transpose(bank[k][:, c * P:(c + 1) * P], otok[:, c, k * P:(k + 1) * P], ident[:, :])
                        m.then_inc(sem("o_turned"), 1)
                    pe.wait_ge(sem("oT_evac"), e0 + KD)
                    projection(pe, seg, oT, tail)

                @block.scalar
                def _(act):
                    projection_squares(act, tail)

                @block.vector
                def _(dve):
                    for k in range(KD):
                        dve.wait_ge(sem("o_turned"), o0 + k + 1)
                        nc.vector.tensor_copy(oT[:, k, :], bank[k]).then_inc(sem("oT_evac"), 1)
                    add_projection(dve, seg, gate)

        def projection_row(pe, seg, src, k):
            w = stream.slot(0).rearrange("p (k c) -> p k c", k=KD)
            if k == 0:
                stream.arrived(pe, seg, 0, 0)
            for t in range(4):
                m = nc.tensor.matmul(bank[t], w[:, k, t * P:(t + 1) * P], src[:, k, :], start=(k == 0), stop=(k == KD - 1))
                if k == KD - 1:
                    m.then_inc(sem("proj_ready" if t < 3 else "unit_done"), 1)

        def projection(pe, seg, src, tail, rows_done=False):
            p0 = counted.get("proj_free", 0)
            for u in range(1 if rows_done else 0, 2):
                stream.arrived(pe, seg, 0, u)
                w = stream.slot(u).rearrange("p (k c) -> p k c", k=KD)
                for t in range(4):
                    if 4 * u + t == 7:
                        pe.wait_ge(sem("proj_free"), p0 + 1)
                    for k in range(KD):
                        m = nc.tensor.matmul(bank[(4 * u + t) % 7], w[:, k, t * P:(t + 1) * P], src[:, k, :], start=(k == 0), stop=(k == KD - 1))
                    m.then_inc(sem("proj_ready" if t < 3 else "unit_done"), 1)
                    if rows_done and t == 0:
                        for k in range(3):
                            tail.sum(pe, k)
                    if u or t:
                        tail.sum(pe, 4 * u + t - 1)
            tail.sum(pe, KD - 1)

        def projection_squares(act, tail):
            p0 = counted.get("proj_free", 0)
            for k in range(KD):
                act.wait_ge(sem("proj_free"), p0 + k + 1)
                tail.square(act, k)

        def add_projection(dve, seg, gate):
            r0 = base("proj_ready", 6)
            base("proj_free", KD)
            for u in range(2):
                for t in range(4):
                    n = 4 * u + t
                    if t < 3:
                        dve.wait_ge(sem("proj_ready"), r0 + 3 * u + t + 1)
                    else:
                        stream.used_up(dve, seg, u)
                    x = xT[:, n, :]
                    if gate is None:
                        ins = nc.vector.tensor_tensor(x, x, bank[n % 7], ALU.add)
                    else:
                        ins = nc.vector.scalar_tensor_tensor(out=x, in0=bank[n % 7], scalar=gate(n), in1=x, op0=ALU.mult, op1=ALU.add)
                    ins.then_inc(sem("proj_free"), 1)

        def stage_hyena():
            owned.close()
            x1 = owned.enter_context(nc.sbuf_tensor("hy_x1", [P, KD, T], F32))
            vg = owned.enter_context(nc.sbuf_tensor("hy_signal", [P, KD, T], F32))
            left = arena_words - 2 * KD * T
            projecting = ExitStack()
            hH, hL, wH, wL = fill_arena(projecting, left, ("hy_h_high", [P, KD, T]), ("hy_h_low", [P, KD, T]),
                                        ("hy_w_high", [P, 2, D]), ("hy_w_low", [P, 2, D]))
            zbuf = take(3, T)
            x2, v = take(T), take(T)
            prepare, gains, shifts = modulated(1, 0, 0, "mix_g", KD)
            norm = Norm(xT, hT, KD, D, gains, shifts)
            HW = placed["hy_conv_w"]

            with nc.Block() as block:
                @block.sync
                def _(sp):
                    stream.issue(sp, "hy_in")

                @block.tensor
                def _(pe):
                    pe.sem_inc(sem("hy_bank_free"), 6)
                    norm.pe(pe)
                    pe.wait_ge(sem("hy_h_low"), KD)

                    def unit(u, i, j):
                        for t in range(3):
                            pe.wait_ge(sem("hy_bank_free"), u * 3 + (t + 1))
                            pe.wait_ge(sem("hy_w_low"), u * 3 + (t + 1))
                            b, n = bank[j % 2 * 3 + t], (3 * j + t) % 2
                            for k in range(KD):
                                high, low = wH[:, n, k * P:(k + 1) * P], wL[:, n, k * P:(k + 1) * P]
                                nc.tensor.matmul(b, high, hH[:, k, :], start=(k == 0), stop=False)
                                nc.tensor.matmul(b, high, hL[:, k, :], start=False, stop=False)
                                m = nc.tensor.matmul(b, low, hH[:, k, :], start=False, stop=(k == KD - 1))
                            m.then_inc(sem("hy_made" if t < 2 else "unit_done"), 1)
                    rounds(pe, KD, unit)

                def split_tile(eng, n, part):
                    if n < 3 * KD:
                        raw = stream.slot(n // 3 % SLOTS)[:, n % 3 * D:(n % 3 + 1) * D]
                        if part == 0:
                            stream.arrived(eng, "hy_in", n // 3 // SLOTS, n // 3 % SLOTS)
                            nc.scalar.copy(wH[:, n % 2, :], raw).then_inc(sem("hy_w_high"), 1)
                        else:
                            eng.wait_ge(sem("hy_w_high"), n + 1)
                            nc.vector.tensor_tensor(wL[:, n % 2, :], raw, wH[:, n % 2, :].bitcast(F32), ALU.subtract).then_inc(sem("hy_w_low"), 1)

                def multiplied(eng, u, t):
                    if t < 2:
                        eng.wait_ge(sem("hy_made"), u * 2 + (t + 1))
                    else:
                        stream.used_up(eng, "hy_in", u)

                @block.scalar
                def _(act):
                    for n in range(2):
                        split_tile(act, n, 0)
                    norm.act(act)
                    for k in range(KD):
                        norm.wait(act, k)
                        nc.scalar.copy(hH[:, k, :], hT[:, k, :]).then_inc(sem("hy_h_high"), 1)
                    b0 = placed["hy_b_in"]
                    act.sem_inc(sem("zbuf_free"), 3)
                    for n in range(3 * KD):
                        u, t = n // 3, n % 3
                        multiplied(act, u, t)
                        split_tile(act, n + 2, 0)
                        act.wait_ge(sem("zbuf_free"), n + 1)
                        nc.scalar.activation(zbuf[:, t, :], bank[u % 2 * 3 + t], ACT.Identity, bias=cols[:, u + (b0 + t * KD), :],
                                             scale=1.0).then_inc(sem("hy_bank_free"), 1)

                @block.vector
                def _(dve):
                    dve_chain.begin()
                    for n in range(2):
                        split_tile(dve, n, 1)
                    dve_chain(prepare())
                    norm.dve(dve)
                    for k in range(KD):
                        dve.wait_ge(sem("hy_h_high"), k + 1)
                        nc.vector.tensor_tensor(hL[:, k, :], hT[:, k, :], hH[:, k, :].bitcast(F32), ALU.subtract).then_inc(sem("hy_h_low"), 1)
                    b0 = placed["hy_conv_b"]
                    for n in range(3 * KD):
                        u, t = n // 3, n % 3
                        z = (x1[:, u, :], x2, v)[t]
                        multiplied(dve, u, t)
                        split_tile(dve, n + 2, 1)
                        dve.wait_ge(sem("hy_bank_free"), n + 7)
                        s, at = zbuf[:, t, :], t * KD
                        dve_chain(nc.vector.tensor_scalar(z, s, cols[:, u + (HW + 24 + at), :], cols[:, u + (b0 + at), :], ALU.mult, ALU.add))
                        dve_chain(nc.vector.scalar_tensor_tensor(out=z[:, 1:T], in0=s[:, 0:T - 1], scalar=cols[:, u + (HW + at), :],
                                                                 in1=z[:, 1:T], op0=ALU.mult, op1=ALU.add))
                        nc.vector.scalar_tensor_tensor(out=z[:, 0:T - 1], in0=s[:, 1:T], scalar=cols[:, u + (HW + 48 + at), :],
                                                       in1=z[:, 0:T - 1], op0=ALU.mult, op1=ALU.add).then_inc(sem("zbuf_free"), 1)
                        if t == 2:
                            dve.wait_ge(sem("zbuf_free"), u * 3 + 6)
                            dve_chain(nc.vector.tensor_tensor(vg[:, u, :], x2, v, ALU.mult))
                    dve_chain.stop()

            projecting.close()
            fill_arena(owned, left)
            fwd = take(2, TB, T)
            inv = take(2, TB, T)
            spectrum = take(2, TB, T)
            vtok = take(TB, T)
            w3 = take(2 * D)
            h2 = take(T)
            decay = take(D)
            tcol = take(8, 1)
            flat = spectrum.rearrange("p a b c -> p (a b c)")
            ab = hT[:, :, :].rearrange("p (a b) c -> p a b c", a=2)
            feats, w1, w2 = flat[:, 0:T], flat[:, T:T + 64], flat[:, T + 64:T + 128]
            arg, turns, h1 = flat[:, 2 * T:3 * T], flat[:, 3 * T:4 * T], flat[:, 4 * T:5 * T]
            TWO_PI_1 = 6.28125
            TWO_PI_2 = float(np.float32(round((2 * np.pi - TWO_PI_1) * 2.0 ** 21) / 2.0 ** 21))
            TWO_PI_3 = float(2 * np.pi - TWO_PI_1 - TWO_PI_2)
            ROUND = 1.5 * 2.0 ** 23
            with nc.Block() as block:
                @block.sync
                def _(sp):
                    sp.dma_start(feats[0:33, :], const["hy_z"]).then_inc(sem("mlp_in"), 16)
                    sp.dma_start(w1[0:33, :], inp["hy_f_w1_2"][0]).then_inc(sem("mlp_in"), 16)
                    sp.dma_start(w2[0:64, :], inp["hy_f_w2_2"][0]).then_inc(sem("mlp_in"), 16)
                    sp.dma_start(tcol, const["hy_t"]).then_inc(sem("hy_tables"), 16)
                    sp.dma_start(w3[0:64, :], inp["hy_f_w3_2"][0]).then_inc(sem("hy_tables"), 16)
                    sp.dma_start(decay, inp["hy_decay_2"][0].partition_broadcast(P)).then_inc(sem("hy_tables"), 16)
                    sp.dma_start(fwd, const["dft"]).then_inc(sem("hy_dft"), 16)
                    sp.dma_start(inv, const["idft"]).then_inc(sem("hy_dft"), 16)

                @block.tensor
                def _(pe):
                    pe.wait_ge(sem("mlp_in"), 48)
                    nc.tensor.matmul(bank[0][0:64, :], w1[0:33, :], feats[0:33, :], start=True, stop=True).then_inc(sem("mlp_made"), 1)
                    pe.wait_ge(sem("mlp_h"), 1)
                    nc.tensor.matmul(bank[1][0:64, :], w2[0:64, :], h1[0:64, :], start=True, stop=True).then_inc(sem("mlp_made"), 1)

                @block.vector
                def _(dve):
                    dve_chain.begin()
                    for n, (b, f) in enumerate((("f_b1", "f_freq1"), ("f_b2", "f_freq2"))):
                        a, k = arg[0:64, :], turns[0:64, :]
                        dve.wait_ge(sem("mlp_made"), n + 1)
                        dve_chain(nc.vector.tensor_scalar(a, bank[n][0:64, :], col(b)[0:64, :], col(f)[0:64, :], ALU.add, ALU.mult))
                        dve_chain(nc.vector.tensor_scalar(k, a, 1.0 / (2 * np.pi), ROUND, ALU.mult, ALU.add))
                        dve_chain(nc.vector.tensor_scalar(k, k, ROUND, None, ALU.subtract))
                        for part in (TWO_PI_1, TWO_PI_2, TWO_PI_3):
                            dve_chain(nc.vector.scalar_tensor_tensor(out=a, in0=k, scalar=-part, in1=a, op0=ALU.mult, op1=ALU.add))
                        nc.vector.tensor_scalar(a, a, -3.1415925, 3.1415925, ALU.max, ALU.min).then_inc(sem("mlp_arg"), 1)
                        dve.wait_ge(sem("mlp_h"), n + 1)
                    dve_chain.stop()

                @block.scalar
                def _(act):
                    for n, h in enumerate((h1, h2)):
                        act.wait_ge(sem("mlp_arg"), n + 1)
                        nc.scalar.activation(h[0:64, :], arg[0:64, :], ACT.Sin).then_inc(sem("mlp_h"), 1)
                    act.wait_ge(sem("hy_tables"), 48)
                    nc.scalar.activation(decay, decay, ACT.Abs).then_inc(sem("decay_abs"), 1)

            HC = KD // 2
            win, t1, t2 = rstd, rstd[:, 0, :], rstd[:, 1, :]
            with nc.Block() as block:
                @block.sync
                def _(sp):
                    pass

                @block.tensor
                def _(pe):
                    for hh in range(2):
                        if hh:
                            pe.wait_ge(sem("y_made"), 4)
                            pe.wait_ge(sem("gated"), 4)
                        for c in range(TB):
                            for d in range(2):
                                m = nc.tensor.matmul(bank[2 * c + d], h2[0:64, c * P:(c + 1) * P], w3[0:64, d * D + hh * T:d * D + (hh + 1) * T], start=True, stop=True)
                            m.then_inc(sem("taps_ready"), 1)
                        pe.wait_ge(sem("taps_done"), 4 * hh + 4)
                        if hh == 0:
                            pe.wait_ge(sem("hy_dft"), 32)
                        for f in range(TB):
                            for d in range(2):
                                for c in range(TB):
                                    m = nc.tensor.matmul(bank[2 * f + d], fwd[:, d, c, f * P:(f + 1) * P], ab[:, d, c, :], start=(c == 0), stop=(c == TB - 1))
                                m.then_inc(sem("spectrum_ready"), 1)
                        for c in range(TB):
                            pe.wait_ge(sem("spectrum_evac"), 8 * hh + c + 1)
                            for k in range(HC):
                                m = nc.tensor.transpose(bank[c][:, k * P:(k + 1) * P], vg[:, HC * hh + k, c * P:(c + 1) * P], ident[:, :])
                            m.then_inc(sem("signal_ready"), 1)
                        pe.wait_ge(sem("spectrum_evac"), 8 * hh + 8)
                        pe.wait_ge(sem("signal_evac"), 4 * hh + 4)
                        for f in range(TB):
                            for d in range(2):
                                for c in range(TB):
                                    m = nc.tensor.matmul(bank[2 * f + d], fwd[:, d, c, f * P:(f + 1) * P], vtok[:, c, :], start=(c == 0), stop=(c == TB - 1))
                            m.then_inc(sem("transformed"), 1)
                        pe.wait_ge(sem("y_made"), 4 * hh + 4)
                        for k in range(HC):
                            for f in range(TB):
                                for d in range(2):
                                    m = nc.tensor.matmul(bank[k], ab[:, d, f, k * P:(k + 1) * P], inv[:, d, f, :], start=(f == 0 and d == 0), stop=(f == TB - 1 and d == 1))
                            m.then_inc(sem("inverted"), 1)

                @block.scalar
                def _(act):
                    for hh in range(2):
                        for c in range(TB):
                            n = 4 * hh + c
                            if n >= 2:
                                act.wait_ge(sem("taps_done"), n - 1)
                            if hh:
                                act.wait_ge(sem("y_made"), 4)
                            nc.scalar.activation(win[:, c % 2, :], decay[:, hh * T:(hh + 1) * T], ACT.Exp, scale=tcol[:, c, :]).then_inc(sem("window"), 1)
                        for f in range(TB):
                            for d in range(2):
                                n = 8 * hh + 2 * f + d
                                act.wait_ge(sem("spectrum_ready"), n + 1)
                                if hh:
                                    act.wait_ge(sem("y_made"), 4)
                                nc.scalar.copy(spectrum[:, d, f, :], bank[2 * f + d]).then_inc(sem("spectrum_evac"), 1)
                        for c in range(TB):
                            act.wait_ge(sem("signal_ready"), 4 * hh + c + 1)
                            nc.scalar.copy(vtok[:, c, :], bank[c]).then_inc(sem("signal_evac"), 1)

                @block.vector
                def _(dve):
                    dve_chain.begin()
                    for hh in range(2):
                        for c in range(TB):
                            n = 4 * hh + c
                            dve.wait_ge(sem("taps_ready"), n + 1)
                            dve.wait_ge(sem("window"), n + 1)
                            w, fw, bw = win[:, c % 2, :], ab[:, 0, c, :], ab[:, 1, c, :]
                            if hh and c == 0:
                                dve.wait_ge(sem("inverted"), 4)
                            dve_chain(nc.vector.scalar_tensor_tensor(out=vtok[:, 0, :], in0=bank[2 * c + 1], scalar=tcol[:, 4 if c == 0 else 5, :], in1=w, op0=ALU.mult, op1=ALU.mult))
                            dve_chain(nc.vector.tensor_tensor(vtok[:, 1, :], w, bank[2 * c], ALU.mult))
                            nc.vector.tensor_tensor(fw, vtok[:, 1, :], vtok[:, 0, :], ALU.add)
                            nc.vector.tensor_tensor(bw, vtok[:, 1, :], vtok[:, 0, :], ALU.subtract).then_inc(sem("taps_done"), 1)
                            dve.wait_ge(sem("taps_done"), n + 1)
                        dve.wait_ge(sem("spectrum_evac"), 8 * hh + 8)
                        for f in range(TB):
                            dve.wait_ge(sem("transformed"), 4 * hh + f + 1)
                            ur, ui = bank[2 * f], bank[2 * f + 1]
                            fr, fi = spectrum[:, 0, f, :], spectrum[:, 1, f, :]
                            yr, yi = ab[:, 0, f, :], ab[:, 1, f, :]
                            nc.vector.tensor_tensor(yr, fr, ur, ALU.mult)
                            nc.vector.tensor_tensor(t1, fi, ui, ALU.mult)
                            nc.vector.tensor_tensor(yi, fi, ur, ALU.mult)
                            dve_chain(nc.vector.tensor_tensor(t2, fr, ui, ALU.mult))
                            nc.vector.tensor_tensor(yr, yr, t1, ALU.subtract)
                            nc.vector.tensor_tensor(yi, yi, t2, ALU.add).then_inc(sem("y_made"), 1)
                            dve.wait_ge(sem("y_made"), 4 * hh + f + 1)
                        for k in range(HC):
                            m = HC * hh + k
                            dve.wait_ge(sem("inverted"), m + 1)
                            dve_chain(nc.vector.scalar_tensor_tensor(out=vg[:, m, :], in0=vg[:, m, :], scalar=cols[:, placed["hy_d"] + m, :], in1=bank[k], op0=ALU.mult, op1=ALU.add))
                            nc.vector.tensor_tensor(vg[:, m, :], vg[:, m, :], x1[:, m, :], ALU.mult).then_inc(sem("gated"), 1)
                    dve_chain.stop()

            gb = tcol
            tail = sums_ahead(hT)
            with nc.Block() as block:
                @block.sync
                def _(sp):
                    stream.issue(sp, "hy_out")

                @block.tensor
                def _(pe):
                    projection(pe, "hy_out", vg, tail)

                @block.scalar
                def _(act):
                    projection_squares(act, tail)

                @block.vector
                def _(dve):
                    dve_chain.begin()
                    dve_chain(nc.vector.tensor_tensor(gb[:, :, 0], modc[:, 1, 2 * KD:3 * KD, 0], cols2("hy_b_out", 0, KD), ALU.mult))
                    for k in range(KD):
                        ins = nc.vector.tensor_scalar(xT[:, k, :], xT[:, k, :], gb[:, k, :], None, ALU.add)
                    dve_chain(ins)
                    add_projection(dve, "hy_out", lambda u: gate_of(1, 0, u))
                    dve_chain.stop()

        C, DK, LEVELS = P, P, 7

        def stage_gdn():
            clear_arena()
            qT, kT, vT, zT = take(GH, T), take(GH, T), take(GH, T), take(GH, T)
            mark = arena_use[0]
            y = take(3, T)
            act_out = take(2, T)
            squares = take(2, T)
            wab = take(KD, 2 * GH)
            raw = take(TB, 2 * GH)
            pos, soft, alog, dtb = take(TB, GH), take(TB, GH), take(GH), take(GH)
            keep = arena_words - 4 * TB * GH - 2 * C - LEVELS * C
            arena_use[0] = keep
            g, beta = take(TB, GH), take(TB, GH)
            tri = take(C)
            levels = take(LEVELS, C)
            norm = Norm(xT, hT, KD, D, lambda k: col("norm_mix", k))
            CW = placed["gdn_conv"]

            with nc.Block() as block:
                @block.sync
                def _(sp):
                    sp.dma_start(wab, inp["gdn_w_in"][0].rearrange("(k p) c -> p k c", p=P)[:, :, 4 * D:4 * D + 2 * GH]).then_inc(sem("gdn_in"), 16)
                    sp.dma_start(alog, inp["gdn_a_log"][0].partition_broadcast(P)).then_inc(sem("gdn_in"), 16)
                    sp.dma_start(dtb, inp["gdn_dt_bias"][0].partition_broadcast(P)).then_inc(sem("gdn_in"), 16)
                    sp.dma_start(tri, const["tri"]).then_inc(sem("gdn_in"), 16)
                    sp.dma_start(levels, const["levels"]).then_inc(sem("gdn_in"), 16)
                    stream.issue(sp, "gdn_in")

                @block.tensor
                def _(pe):
                    pe.sem_inc(sem("q_convolved"), 2)
                    pe.sem_inc(sem("k_convolved"), 2)
                    pe.sem_inc(sem("v_convolved"), 1)
                    pe.sem_inc(sem("z_done"), 1)
                    pe.sem_inc(sem("l2_rooted"), 2)
                    norm.pe(pe)
                    norm.wait(pe)
                    pe.wait_ge(sem("gdn_in"), 80)
                    for c in range(TB):
                        for k in range(KD):
                            m = nc.tensor.matmul(bank[6][:, c * 16:(c + 1) * 16], hT[:, k, c * P:(c + 1) * P], wab[:, k, :], start=(k == 0), stop=(k == KD - 1))
                    m.then_inc(sem("ab_ready"), 1)
                    pe.wait_ge(sem("ab_read"), 1)

                    def unit(u, i, j):
                        stream.arrived(pe, "gdn_in", i, j)
                        w = stream.slot(j).rearrange("p (t k c) -> p t k c", t=4, k=KD)

                        def product(t, b):
                            for k in range(KD):
                                m = nc.tensor.matmul(bank[b], w[:, t, k, :], hT[:, k, :], start=(k == 0), stop=(k == KD - 1))
                            return m
                        pe.wait_ge(sem("q_convolved"), u + 1)
                        product(0, j % 2).then_inc(sem("gdn_made"), 1)
                        pe.wait_ge(sem("k_convolved"), u + 1)
                        product(1, 2 + j % 2).then_inc(sem("gdn_made"), 1)
                        pe.wait_ge(sem("z_done"), u + 1)
                        product(3, 4).then_inc(sem("gdn_made"), 1)
                        for t in range(2):
                            pe.wait_ge(sem("l2_squares"), u * 2 + (t + 1))
                            pe.wait_ge(sem("l2_rooted"), u * 2 + (t + 1))
                            nc.tensor.matmul(bank[6 + t], ones[:, :], squares[:, t, :], start=True, stop=True).then_inc(sem("l2_summed"), 1)
                        pe.wait_ge(sem("v_convolved"), u + 1)
                        product(2, 5).then_inc(sem("unit_done"), 1)
                    rounds(pe, GH, unit)

                @block.scalar
                def _(act):
                    act.sem_inc(sem("l2_normed"), 2)
                    norm.act(act)
                    act.wait_ge(sem("gate_args"), 1)
                    act_chain.begin()
                    act_chain(nc.scalar.activation(soft, soft, ACT.Exp))
                    act_chain(nc.scalar.activation(alog, alog, ACT.Exp))
                    nc.scalar.activation(soft, soft, ACT.Ln, bias=ones[:, 0:1]).then_inc(sem("gate_parts"), 1)
                    act_chain(nc.scalar.activation(beta, raw[:, :, GH:2 * GH], ACT.Sigmoid))
                    act_chain.stop()

                    def unit(u, i, j):
                        act_chain.unit(u, 2)
                        for t, name in enumerate(("q_convolved", "k_convolved")):
                            act.wait_ge(sem(name), u + 3)
                            act.wait_ge(sem("l2_normed"), u * 2 + (t + 1))
                            act_chain(nc.scalar.activation(act_out[:, t, :], y[:, t, :], ACT.Silu))
                            nc.scalar.activation(squares[:, t, :], act_out[:, t, :], ACT.Square).then_inc(sem("l2_squares"), 1)
                        act.wait_ge(sem("gdn_made"), u * 3 + 3)
                        nc.scalar.activation(zT[:, u, :], bank[4], ACT.Silu).then_inc(sem("z_done"), 1)
                        for t in range(2):
                            act.wait_ge(sem("l2_summed"), u * 2 + (t + 1))
                            nc.scalar.activation(rstd[:, t, :], bank[6 + t], ACT.Sqrt, bias=eps_col[:, :], scale=1.0).then_inc(sem("l2_rooted"), 1)
                        act.wait_ge(sem("v_convolved"), u + 2)
                        nc.scalar.activation(vT[:, u, :], y[:, 2, :], ACT.Silu).then_inc(sem("v_silu"), 1)
                    rounds(act, GH, unit)
                    act_chain.end(GH)

                @block.vector
                def _(dve):
                    dve_chain.begin()
                    norm.dve(dve)
                    dve.wait_ge(sem("gdn_in"), 80)
                    dve.wait_ge(sem("ab_ready"), 1)
                    nc.vector.tensor_copy(raw, bank[6][:, 0:TB * 2 * GH].rearrange("p (c h) -> p c h", c=TB)).then_inc(sem("ab_read"), 1)
                    dve.wait_ge(sem("ab_read"), 1)
                    dve_chain(nc.vector.tensor_tensor(pos, raw[:, :, 0:GH], bcast(dtb, 1, TB), ALU.add))
                    dve_chain(nc.vector.tensor_scalar(soft, pos, -1.0, None, ALU.mult))
                    dve_chain(nc.vector.tensor_tensor(soft, pos, soft, ALU.min))
                    nc.vector.tensor_scalar(pos, pos, 0.0, None, ALU.max).then_inc(sem("gate_args"), 1)
                    dve.wait_ge(sem("gate_args"), 1)
                    dve.wait_ge(sem("gate_parts"), 1)
                    dve_chain(nc.vector.tensor_tensor(pos, pos, soft, ALU.add))
                    dve_chain(nc.vector.tensor_tensor(pos, pos, bcast(alog, 1, TB), ALU.mult))
                    dve_chain(nc.vector.tensor_scalar(g, pos, -1.0, None, ALU.mult))
                    dve_chain.stop()

                    def unit(u, i, j):
                        dve_chain.unit(u, 3 * 3 + 2)

                        def convolve(t, b, name):
                            z = y[:, t, :]
                            dve_chain(nc.vector.tensor_scalar(z, b, cols[:, u + (CW + 72 + 8 * t), :], None, ALU.mult))
                            for lag in range(1, 4):
                                ins = nc.vector.scalar_tensor_tensor(out=z[:, lag:T], in0=b[:, 0:T - lag], scalar=cols[:, u + (CW + 24 * (3 - lag) + 8 * t), :],
                                                                     in1=z[:, lag:T], op0=ALU.mult, op1=ALU.add)
                                if lag < 3:
                                    dve_chain(ins)
                            ins.then_inc(sem(name), 1)
                        dve.wait_ge(sem("gdn_made"), u * 3 + 1)
                        convolve(0, bank[j % 2], "q_convolved")
                        dve.wait_ge(sem("gdn_made"), u * 3 + 2)
                        convolve(1, bank[2 + j % 2], "k_convolved")
                        for t, (dst, s) in enumerate(((qT, DK ** -0.5), (kT, 1.0))):
                            dve.wait_ge(sem("l2_rooted"), u * 2 + (t + 3))
                            rs = rstd[:, t, :]
                            dve_chain(nc.vector.reciprocal(rs, rs))
                            nc.vector.scalar_tensor_tensor(out=dst[:, u, :], in0=act_out[:, t, :], scalar=s, in1=rs, op0=ALU.mult, op1=ALU.mult).then_inc(sem("l2_normed"), 1)
                        stream.used_up(dve, "gdn_in", u)
                        convolve(2, bank[5], "v_convolved")
                    rounds(dve, GH, unit)
                    dve_chain.end(GH)

            arena_use[0] = mark

            def heads(v):
                return v.rearrange("p (h t) -> p h t", h=GH)
            spare = [hT[:, 2 * n:2 * n + 2, :].rearrange("p a b -> p (a b)") for n in range(4)]
            kc, ktail, vb, decay = (heads(v) for v in spare)
            grow, NL, L, T1, X, XT, S = (heads(take(GH * C)) for _ in range(7))
            qdec, R, VN, vc, TG, IB = grow, L, X, L, T1, NL
            gcol, egc, tail, cdec, nbe = take(GH), take(GH), take(GH), take(GH), take(GH)
            assert arena_use[0] <= keep

            def pair(b):
                return psum[:, b:b + 2, :].rearrange("p a (h t) -> p (a h) t", t=C)

            def chunk(v, c):
                return v.rearrange("p h (c t) -> p c h t", t=C)[:, c, :, :]
            tri_h, ident_h = bcast(tri, 1, GH), bcast(ident[:, :], 1, GH)
            HALF = GH // 2

            with nc.Block() as block:
                @block.gpsimd
                def _(pool):
                    pool.sem_inc(sem("chunk_done"), 1)
                    nc.gpsimd.memset(S, 0.0).then_inc(sem("state_clear"), 1)
                    with pool.Fori(0, TB) as c:
                        pool.wait_ge(sem("chunk_done"), c + 1)
                        nc.gpsimd.tensor_copy(kc, chunk(kT, c)).then_inc(sem("kc_ready"), 1)
                        nc.gpsimd.tensor_copy(vc, chunk(vT, c)).then_inc(sem("vc_ready"), 1)
                        pool.wait_ge(sem("row_exp"), c * 2 + 2)
                        nc.gpsimd.tensor_tensor(qdec, grow, chunk(qT, c), ALU.mult).then_inc(sem("qdec_ready"), 1)
                        for lv in range(LEVELS):
                            if lv == 0:
                                pool.wait_ge(sem("a_ready"), c + 1)
                            else:
                                pool.wait_ge(sem("LX_ready"), c * (2 * LEVELS) + 2 * lv)
                                pool.wait_ge(sem("XT_ready"), c * (2 * LEVELS) + 2)
                            nc.gpsimd.tensor_tensor(L, NL, bcast(levels[:, lv, :], 1, GH), ALU.mult).then_inc(sem("L_ready"), 1)

                @block.tensor
                def _(pe):
                    with pe.Fori(0, TB) as c:
                        pe.wait_ge(sem("kc_ready"), c + 1)
                        nc.tensor.matmul(bank[0][:, 0:GH], tri, g[:, c, :], start=True, stop=True).then_inc(sem("gcol_ready"), 1)
                        pe.wait_ge(sem("vc_ready"), c + 1)
                        for h in range(GH):
                            m = nc.tensor.transpose(pair(2)[:, h, :], vc[:, h, :], ident[:, :])
                        m.then_inc(sem("vtok_ready"), 1)
                        for b, src in ((4, TG), (6, IB)):
                            pe.wait_ge(sem("masked_ready"), c * 2 + (1 if b == 4 else 2))
                            for a in range(2):
                                m = nc.tensor.matmul(bank[b + a], ones[:, :], src[:, a * HALF:(a + 1) * HALF, :].rearrange("p h t -> p (h t)"), start=True, stop=True)
                            m.then_inc(sem("row_ready"), 1)
                        pe.wait_ge(sem("gcol_evac"), c + 1)
                        for h in range(GH):
                            m = nc.tensor.transpose(pair(0)[:, h, :], kc[:, h, :], ident[:, :])
                        m.then_inc(sem("ktok_ready"), 1)
                        pe.wait_ge(sem("row_exp"), c * 2 + 2)
                        pe.wait_ge(sem("cdec_ready"), c + 1)
                        for h in range(GH):
                            m = nc.tensor.matmul(pair(4)[:, h, :], kc[:, h, :], kc[:, h, :], start=True, stop=True)
                        m.then_inc(sem("kk_ready"), 1)
                        pe.wait_ge(sem("beta_used"), c + 1)
                        for h in range(GH):
                            m = nc.tensor.matmul(pair(6)[:, h, :], kc[:, h, :], chunk(qT, c)[:, h, :], start=True, stop=True)
                        m.then_inc(sem("kq_ready"), 1)
                        for lv in range(LEVELS):
                            pe.wait_ge(sem("L_ready"), c * LEVELS + lv + 1)
                            if lv == 0:
                                pe.wait_ge(sem("ktail_ready"), c + 1)
                            for a in range(2):
                                if lv:
                                    pe.wait_ge(sem("XT_ready"), c * (2 * LEVELS) + 2 * (lv - 1) + a + 1)
                                for h in range(a * HALF, (a + 1) * HALF):
                                    if lv == 0:
                                        m = nc.tensor.transpose(pair(0)[:, h, :], L[:, h, :], ident[:, :])
                                    else:
                                        m = nc.tensor.matmul(pair(0)[:, h, :], L[:, h, :], X[:, h, :], start=True, stop=True)
                                m.then_inc(sem("LX_ready"), 1)
                            if lv == 0:
                                continue
                            for a in range(2):
                                pe.wait_ge(sem("T1_ready"), c * (2 * LEVELS - 2) + 2 * (lv - 1) + a + 1)
                                if lv < LEVELS - 1:
                                    for h in range(a * HALF, (a + 1) * HALF):
                                        m = nc.tensor.matmul(pair(2)[:, h, :], XT[:, h, :], T1[:, h, :], start=True, stop=True)
                                    m.then_inc(sem("dX_ready"), 1)
                                for h in range(a * HALF, (a + 1) * HALF):
                                    m = nc.tensor.matmul(pair(4)[:, h, :], T1[:, h, :], XT[:, h, :], start=True, stop=True)
                                m.then_inc(sem("dXT_ready"), 1)
                        pe.wait_ge(sem("kq_used"), c + 1)
                        for a in range(2):
                            for h in range(a * HALF, (a + 1) * HALF):
                                m = nc.tensor.matmul(pair(6)[:, h, :], kc[:, h, :], S[:, h, :], start=True, stop=True)
                            m.then_inc(sem("kS_ready"), 1)
                        for a in range(2):
                            pe.wait_ge(sem("R_ready"), c * 2 + (a + 1))
                            pe.wait_ge(sem("XT_ready"), c * (2 * LEVELS) + 2 * (LEVELS - 1) + a + 1)
                            for h in range(a * HALF, (a + 1) * HALF):
                                m = nc.tensor.matmul(pair(0)[:, h, :], XT[:, h, :], R[:, h, :], start=True, stop=True)
                            m.then_inc(sem("v_made"), 1)
                        pe.wait_ge(sem("qdec_ready"), c + 1)
                        for a in range(2):
                            pe.wait_ge(sem("V_ready"), c * 2 + (a + 1))
                            for h in range(a * HALF, (a + 1) * HALF):
                                nc.tensor.matmul(pair(2)[:, h, :], S[:, h, :], qdec[:, h, :], start=True, stop=False)
                                m = nc.tensor.matmul(pair(2)[:, h, :], VN[:, h, :], decay[:, h, :], start=False, stop=True)
                            m.then_inc(sem("out_made"), 1)
                            for h in range(a * HALF, (a + 1) * HALF):
                                m = nc.tensor.matmul(pair(4)[:, h, :], ktail[:, h, :], VN[:, h, :], start=True, stop=True)
                            m.then_inc(sem("dS_ready"), 1)

                @block.scalar
                def _(act):
                    with act.Fori(0, TB) as c:
                        act.wait_ge(sem("gcol_evac"), c + 1)
                        nc.scalar.activation(egc, gcol, ACT.Exp).then_inc(sem("col_exp"), 1)
                        act.wait_ge(sem("diff_ready"), c + 1)
                        nc.scalar.activation(decay, decay, ACT.Exp).then_inc(sem("row_exp"), 1)
                        act.wait_ge(sem("last_ready"), c + 1)
                        nc.scalar.activation(grow, pair(4), ACT.Exp).then_inc(sem("row_exp"), 1)
                        nc.scalar.activation(tail, tail, ACT.Exp).then_inc(sem("col_exp"), 1)
                        nc.scalar.activation(cdec, pair(4)[:, :, C - 1], ACT.Exp).then_inc(sem("cdec_ready"), 1)
                        for lv in range(1, LEVELS):
                            for a in range(2):
                                act.wait_ge(sem("LX_ready"), c * (2 * LEVELS) + 2 * lv + a + 1)
                                nc.scalar.copy(T1[:, a * HALF:(a + 1) * HALF, :], pair(0)[:, a * HALF:(a + 1) * HALF, :]).then_inc(sem("T1_ready"), 1)
                        for a in range(2):
                            act.wait_ge(sem("v_made"), c * 2 + (a + 1))
                            nc.scalar.copy(VN[:, a * HALF:(a + 1) * HALF, :], pair(0)[:, a * HALF:(a + 1) * HALF, :]).then_inc(sem("V_ready"), 1)
                        for a in range(2):
                            act.wait_ge(sem("out_made"), c * 2 + (a + 1))
                            nc.scalar.copy(chunk(qT, c)[:, a * HALF:(a + 1) * HALF, :], pair(2)[:, a * HALF:(a + 1) * HALF, :]).then_inc(sem("out_evac"), 1)

                @block.vector
                def _(dve):
                    dve.wait_ge(sem("state_clear"), 1)
                    LINKS = 4 + 2 + 2 + 3
                    with dve.Fori(0, TB) as c:
                        dve_chain.unit(c, LINKS)
                        dve.wait_ge(sem("kc_ready"), c + 1)
                        nc.vector.tensor_tensor(TG, tri_h, bcast(g[:, c, :], 2, C), ALU.mult).then_inc(sem("masked_ready"), 1)
                        nc.vector.tensor_tensor(IB, ident_h, bcast(beta[:, c, :], 2, C), ALU.mult).then_inc(sem("masked_ready"), 1)
                        dve.wait_ge(sem("gcol_ready"), c + 1)
                        nc.vector.tensor_copy(gcol, bank[0][:, 0:GH]).then_inc(sem("gcol_evac"), 1)
                        dve.wait_ge(sem("gcol_evac"), c + 1)
                        dve.wait_ge(sem("row_ready"), c * 2 + 1)
                        dve_chain(nc.vector.tensor_tensor(decay, pair(4), bcast(gcol, 2, C), ALU.subtract))
                        nc.vector.tensor_scalar(decay, decay, 0.0, None, ALU.min).then_inc(sem("diff_ready"), 1)
                        nc.vector.tensor_tensor(tail, pair(4)[:, :, C - 1], gcol, ALU.subtract).then_inc(sem("last_ready"), 1)
                        dve.wait_ge(sem("vtok_ready"), c + 1)
                        dve_chain(nc.vector.tensor_tensor(vb, pair(2), bcast(beta[:, c, :], 2, C), ALU.mult))
                        dve.wait_ge(sem("row_exp"), c * 2 + 1)
                        dve_chain(nc.vector.tensor_tensor(decay, decay, tri_h, ALU.mult))
                        dve.wait_ge(sem("row_ready"), c * 2 + 2)
                        nc.vector.scalar_tensor_tensor(out=NL, in0=pair(6), scalar=-1.0, in1=decay, op0=ALU.mult, op1=ALU.mult).then_inc(sem("beta_used"), 1)
                        dve.wait_ge(sem("beta_used"), c + 1)
                        dve.wait_ge(sem("kk_ready"), c + 1)
                        nc.vector.tensor_tensor(NL, NL, pair(4), ALU.mult).then_inc(sem("a_ready"), 1)
                        dve.wait_ge(sem("col_exp"), c * 2 + 2)
                        dve.wait_ge(sem("ktok_ready"), c + 1)
                        nc.vector.tensor_tensor(ktail, pair(0), bcast(tail, 2, C), ALU.mult).then_inc(sem("ktail_ready"), 1)
                        dve.wait_ge(sem("kq_ready"), c + 1)
                        nc.vector.tensor_tensor(decay, decay, pair(6), ALU.mult).then_inc(sem("kq_used"), 1)
                        dve_chain(nc.vector.scalar_tensor_tensor(out=nbe, in0=egc, scalar=-1.0, in1=beta[:, c, :], op0=ALU.mult, op1=ALU.mult))
                        dve.wait_ge(sem("row_exp"), c * 2 + 2)
                        dve.wait_ge(sem("L_ready"), c * LEVELS + 1)
                        for lv in range(LEVELS):
                            for a in range(2):
                                s = slice(a * HALF, (a + 1) * HALF)
                                if lv == 0:
                                    dve.wait_ge(sem("LX_ready"), c * (2 * LEVELS) + a + 1)
                                    dve_chain(nc.vector.tensor_tensor(X[:, s, :], pair(0)[:, s, :], ident_h[:, s, :], ALU.add))
                                    nc.vector.tensor_tensor(XT[:, s, :], L[:, s, :], ident_h[:, s, :], ALU.add).then_inc(sem("XT_ready"), 1)
                                    continue
                                if lv < LEVELS - 1:
                                    dve.wait_ge(sem("dX_ready"), c * (2 * LEVELS - 4) + 2 * (lv - 1) + a + 1)
                                    nc.vector.tensor_tensor(X[:, s, :], X[:, s, :], pair(2)[:, s, :], ALU.add)
                                dve.wait_ge(sem("dXT_ready"), c * (2 * LEVELS - 2) + 2 * (lv - 1) + a + 1)
                                nc.vector.tensor_tensor(XT[:, s, :], XT[:, s, :], pair(4)[:, s, :], ALU.add).then_inc(sem("XT_ready"), 1)
                        dve.wait_ge(sem("XT_ready"), c * (2 * LEVELS) + 2 * LEVELS)
                        for a in range(2):
                            s = slice(a * HALF, (a + 1) * HALF)
                            dve.wait_ge(sem("kS_ready"), c * 2 + (a + 1))
                            dve_chain(nc.vector.tensor_tensor(R[:, s, :], pair(6)[:, s, :], bcast(nbe[:, s], 2, C), ALU.mult))
                            nc.vector.tensor_tensor(R[:, s, :], R[:, s, :], vb[:, s, :], ALU.add).then_inc(sem("R_ready"), 1)
                        for a in range(2):
                            s = slice(a * HALF, (a + 1) * HALF)
                            dve.wait_ge(sem("dS_ready"), c * 2 + (a + 1))
                            dve.wait_ge(sem("cdec_ready"), c + 1)
                            dve_chain(nc.vector.tensor_tensor(S[:, s, :], S[:, s, :], bcast(cdec[:, s], 2, C), ALU.mult))
                            ins = nc.vector.tensor_tensor(S[:, s, :], S[:, s, :], pair(4)[:, s, :], ALU.add)
                            if a == 0:
                                dve_chain(ins)
                        ins.then_inc(sem("state_ready"), 1)
                        dve.wait_ge(sem("out_evac"), c * 2 + 2)
                        dve.wait_ge(sem("state_ready"), c + 1)
                        nc.vector.tensor_copy(cdec, cdec).then_inc(sem("chunk_done"), 1)
                    dve_chain.end(TB)

            arena_use[0] = mark
            sq = take(2, T)
            tail = sums_ahead(hT)
            with nc.Block() as block:
                @block.sync
                def _(sp):
                    stream.issue(sp, "gdn_out")

                def root(act, h):
                    act.wait_ge(sem("on_summed"), h + 1)
                    if h >= 2:
                        act.wait_ge(sem("on_scaled"), h - 1)
                    nc.scalar.activation(rstd[:, h % 2, :], bank[6 + h % 2], ACT.Sqrt, bias=eps_col[:, :], scale=1.0 / DK).then_inc(sem("on_rooted"), 1)

                @block.scalar
                def _(act):
                    for h in range(GH):
                        if h >= 2:
                            act.wait_ge(sem("on_summed"), h - 1)
                        nc.scalar.activation(sq[:, h % 2, :], qT[:, h, :], ACT.Square).then_inc(sem("on_squares"), 1)
                        if h:
                            root(act, h - 1)
                    root(act, GH - 1)
                    projection_squares(act, tail)

                @block.tensor
                def _(pe):
                    def project_head(h):
                        pe.wait_ge(sem("on_ready"), h + 1)
                        projection_row(pe, "gdn_out", qT, h)

                    for h in range(GH):
                        pe.wait_ge(sem("on_squares"), h + 1)
                        if h >= 2:
                            pe.wait_ge(sem("on_rooted"), h - 1)
                        nc.tensor.matmul(bank[6 + h % 2], ones[:, :], sq[:, h % 2, :], start=True, stop=True).then_inc(sem("on_summed"), 1)
                        if h >= 2:
                            project_head(h - 2)
                    for h in range(GH - 2, GH):
                        project_head(h)
                    projection(pe, "gdn_out", qT, tail, rows_done=True)

                @block.vector
                def _(dve):
                    dve_chain.begin()
                    for h in range(GH):
                        dve.wait_ge(sem("on_rooted"), h + 1)
                        rs = rstd[:, h % 2, :]
                        dve_chain(nc.vector.reciprocal(rs, rs))
                        nc.vector.scalar_tensor_tensor(out=qT[:, h, :], in0=qT[:, h, :], scalar=col("gdn_norm"), in1=rs, op0=ALU.mult, op1=ALU.mult).then_inc(sem("on_scaled"), 1)
                        dve.wait_ge(sem("on_scaled"), h + 1)
                        nc.vector.tensor_tensor(qT[:, h, :], qT[:, h, :], zT[:, h, :], ALU.mult).then_inc(sem("on_ready"), 1)
                    dve_chain.stop()
                    add_projection(dve, "gdn_out", None)

        DH, GROUPS, RES, PAIRS = 64, 3, 4, 4

        def stage_dilated():
            clear_arena()
            q_new, k_new, v_new = take(GROUPS, T), take(GROUPS, T), take(GROUPS, TB, P)
            q_cur, k_cur, v_cur = take(GROUPS, T), take(GROUPS, T), take(GROUPS, TB, P)
            raw, squares, vraw = take(3, T), take(2, T), take(2, T)
            logits, probs, probsT = take(T + 2 * P), take(T + 2 * P), take(T + 2 * P)
            dist = take(RES * T + 2 * P)
            slopes = take(PAIRS, 2 * GROUPS)
            blockones = take(P)
            qgain = take(1)
            stats = take(4)
            otok = take(RES, P)
            oT = take(PAIRS, T)
            norm = Norm(xT, hT, KD, D, lambda k: col("norm_mix", KD + k))
            B_S, B_T, B_O, B_P, B_X = 0, 2, 4, 5, 7
            TILES = 3 * GROUPS
            NQK = 2 * GROUPS

            def by_residue(v):
                return v.rearrange("p (r s) -> p s r", r=RES)

            def tokens(v):
                return v.rearrange("p (s r) -> p s r", r=RES)

            def tiles_of(n):
                return (0, 1) if n == 0 else (n + 1,)

            with nc.Block() as block:
                @block.sync
                def _(sp):
                    sp.dma_start(dist, const["dil_dist"]).then_inc(sem("dil_in"), 16)
                    sp.dma_start(slopes, const["dil_slopes"]).then_inc(sem("dil_in"), 16)
                    sp.dma_start(blockones, const["blockones"]).then_inc(sem("dil_in"), 16)
                    stream.issue(sp, "dil_in")

                @block.tensor
                def _(pe):
                    pe.sem_inc(sem("dil_raw"), 2)

                    def project_tile(t, pr):
                        if t % 3 == 0:
                            stream.arrived(pe, "dil_in", pr, t // 3)
                        pe.wait_ge(sem("dil_raw"), pr * TILES + (2 if t == 0 else t + 1))
                        w = stream.slot(t // 3)[:, 0:3 * D].rearrange("p (g k c) -> p g k c", g=3, k=KD)
                        for k in range(KD):
                            m = nc.tensor.matmul(bank[B_P + t % 2], w[:, t % 3, k, :], hT[:, k, :], start=(k == 0), stop=(k == KD - 1))
                        m.then_inc(sem("unit_done" if t % 3 == 2 else "dil_made"), 1)

                    def follow(t, pr, first=False):
                        if t < NQK:
                            pe.wait_ge(sem("dil_squares"), pr * NQK + (t + 1))
                            if t:
                                pe.wait_ge(sem("dil_rooted"), pr * NQK + t)
                            elif not first:
                                pe.wait_ge(sem("dil_v_evac"), pr * GROUPS)
                            nc.tensor.matmul(bank[B_X], blockones, squares[:, t % 2, :], start=True, stop=True).then_inc(sem("dil_summed"), 1)
                        else:
                            gi = t - NQK
                            pe.wait_ge(sem("dil_raw"), pr * TILES + (t + 3))
                            if gi == 0:
                                pe.wait_ge(sem("dil_rooted"), pr * NQK + NQK)
                            else:
                                pe.wait_ge(sem("dil_v_evac"), pr * GROUPS + gi)
                            for c in range(TB):
                                m = nc.tensor.transpose(bank[B_X][:, c * P:(c + 1) * P], vraw[:, gi % 2, c * P:(c + 1) * P], ident[:, :])
                            m.then_inc(sem("dil_v_turned"), 1)

                    norm.pe(pe)
                    norm.wait(pe)
                    pe.wait_ge(sem("dil_in"), 48)
                    for t in range(TILES):
                        project_tile(t, 0)
                        if t:
                            follow(t - 1, 0, True)
                    follow(TILES - 1, 0)

                    def attend(hp, more):
                        pe.wait_ge(sem("dil_cur"), hp * 2 + 2)
                        for n in range(2 * RES):
                            h, r = n // RES, n % RES
                            it = hp * 8 + n
                            q = q_cur[h * DH:(h + 1) * DH, :, r * P:(r + 1) * P]
                            k = k_cur[h * DH:(h + 1) * DH, :, :]
                            nc.tensor.matmul(bank[B_S], q[:, 0, :], k[:, 0, :], start=True, stop=True)
                            nc.tensor.matmul(bank[B_S + 1][:, 0:P], q[:, 1, :], k[:, 1, r * P:(r + 1) * P], start=True, stop=True)
                            nc.tensor.matmul(bank[B_S + 1][:, P:2 * P], q[:, 2, :], k[:, 2, r * P:(r + 1) * P], start=True, stop=True).then_inc(sem("dil_scores"), 1)
                            if more:
                                for t in tiles_of(n):
                                    project_tile(t, hp + 1)
                            pe.wait_ge(sem("dil_probs"), it + 1)
                            for c in range(6):
                                m = nc.tensor.transpose(bank[B_T + c // 4][:, c % 4 * P:(c % 4 + 1) * P], probs[:, c * P:(c + 1) * P], ident[:, :])
                            m.then_inc(sem("dil_turned"), 1)
                            if more and n:
                                for t in tiles_of(n - 1):
                                    follow(t, hp + 1)
                            pe.wait_ge(sem("dil_low"), it + 1)
                            pe.wait_ge(sem("dil_high"), it + 1)
                            if n == 0:
                                pe.wait_ge(sem("dil_v_cur"), hp + 1)
                            for c in range(6):
                                v = v_cur[:, 0, c, h * DH:(h + 1) * DH] if c < 4 else v_cur[:, c - 3, r, h * DH:(h + 1) * DH]
                                m = nc.tensor.matmul(bank[B_O][:, 0:DH], probsT[:, c * P:(c + 1) * P], v, start=(c == 0), stop=(c == 5))
                            m.then_inc(sem("dil_summed_v"), 1)
                        if more:
                            follow(TILES - 1, hp + 1)
                        pe.wait_ge(sem("dil_o"), hp * 8 + 8)
                        for r in range(RES):
                            m = nc.tensor.transpose(bank[B_T][:, r * P:(r + 1) * P], otok[:, r, :], ident[:, :])
                        m.then_inc(sem("dil_o_turned"), 1)
                    with pe.Fori(0, PAIRS - 1) as hp:
                        attend(hp, True)
                    attend(PAIRS - 1, False)

                @block.gpsimd
                def _(pool):
                    def square(t, pr):
                        pool.wait_ge(sem("dil_raw"), pr * TILES + (t + 3))
                        if t >= 2:
                            pool.wait_ge(sem("dil_summed"), pr * NQK + (t - 1))
                        nc.gpsimd.tensor_tensor(squares[:, t % 2, :], raw[:, t % 3, :], raw[:, t % 3, :], ALU.mult).then_inc(sem("dil_squares"), 1)

                    for t in range(NQK):
                        square(t, 0)
                    with pool.Fori(0, PAIRS - 1) as hp:
                        for t in range(NQK):
                            square(t, hp + 1)

                @block.scalar
                def _(act):
                    def take_raw(t, pr):
                        if t % 3 < 2:
                            act.wait_ge(sem("dil_made"), pr * 6 + (2 * (t // 3) + t % 3 + 1))
                        else:
                            stream.used_up(act, "dil_in", pr * 3 + t // 3)
                        if t < NQK:
                            if t >= 3:
                                act.wait_ge(sem("dil_normed"), pr * NQK + (t - 2))
                            dst, src = raw[:, t % 3, :], bank[B_P + t % 2]
                        else:
                            gi = t - NQK
                            if gi == 2:
                                act.wait_ge(sem("dil_v_turned"), pr * GROUPS + 1)
                            dst, src = vraw[:, gi % 2, :], bank[B_P + t % 2]
                            if gi:
                                dst, src = by_residue(dst), tokens(src)
                        nc.scalar.copy(dst, src).then_inc(sem("dil_raw"), 1)

                    def root(t, pr):
                        if t >= NQK:
                            return
                        act.wait_ge(sem("dil_summed"), pr * NQK + (t + 1))
                        if t >= 2:
                            act.wait_ge(sem("dil_normed"), pr * NQK + (t - 1))
                        nc.scalar.activation(rstd[:, t % 2, :], bank[B_X], ACT.Sqrt, bias=eps_col[:, :], scale=1.0 / DH).then_inc(sem("dil_rooted"), 1)

                    def queries(hp):
                        act.wait_ge(sem("dil_normed"), hp * NQK + NQK)
                        nc.scalar.copy(q_cur, q_new).then_inc(sem("dil_cur"), 1)

                    def values(hp):
                        act.wait_ge(sem("dil_v_evac"), hp * GROUPS + GROUPS)
                        nc.scalar.copy(v_cur, v_new).then_inc(sem("dil_v_cur"), 1)

                    norm.act(act)
                    for t in range(TILES):
                        take_raw(t, 0)
                        if t:
                            root(t - 1, 0)
                    queries(0)
                    values(0)

                    def attend(hp, more):
                        for n in range(2 * RES):
                            it = hp * 8 + n
                            act.wait_ge(sem("dil_max"), it + 1)
                            nc.scalar.activation(probs, logits, ACT.Exp, bias=stats[:, 0:1], scale=1.0, accum_out=stats[:, 1:2]).then_inc(sem("dil_probs"), 1)
                            if more:
                                for t in tiles_of(n):
                                    take_raw(t, hp + 1)
                            act.wait_ge(sem("dil_turned"), it + 1)
                            nc.scalar.copy(probsT[:, T:T + 2 * P], bank[B_T + 1][:, 0:2 * P]).then_inc(sem("dil_high"), 1)
                            if more and n:
                                for t in tiles_of(n - 1):
                                    root(t, hp + 1)
                        if more:
                            queries(hp + 1)
                            act.wait_ge(sem("dil_summed_v"), hp * 8 + 8)
                            values(hp + 1)
                    with act.Fori(0, PAIRS - 1) as hp:
                        attend(hp, True)
                    attend(PAIRS - 1, False)

                @block.vector
                def _(dve):
                    def normalise(t, pr):
                        dve.wait_ge(sem("dil_rooted"), pr * NQK + (t + 1))
                        rs = rstd[:, t % 2, :]
                        dve_chain(nc.vector.reciprocal(rs, rs))
                        g, (dst, gn) = t % 3, ((q_new, qgain) if t < GROUPS else (k_new, col("dil_k")))
                        out_, a, b = dst[:, g, :], raw[:, t % 3, :], rs
                        if t != GROUPS:
                            out_, a, b = by_residue(out_), tokens(a), tokens(b)
                        nc.vector.scalar_tensor_tensor(out=out_, in0=a, scalar=gn, in1=b, op0=ALU.mult, op1=ALU.mult).then_inc(sem("dil_normed"), 1)

                    def values(gi, pr):
                        dve.wait_ge(sem("dil_v_turned"), pr * GROUPS + (gi + 1))
                        nc.vector.tensor_copy(v_new[:, gi, :, :], bank[B_X].rearrange("p (c d) -> p c d", c=TB)).then_inc(sem("dil_v_evac"), 1)

                    def follow(t, pr):
                        normalise(t, pr) if t < NQK else values(t - NQK, pr)

                    def keys(hp):
                        dve.wait_ge(sem("dil_normed"), hp * NQK + NQK)
                        nc.vector.tensor_copy(k_cur, k_new).then_inc(sem("dil_cur"), 1)

                    dve_chain.begin()
                    norm.dve(dve)
                    dve_chain(nc.vector.tensor_scalar(qgain, col("dil_q"), DH ** -0.5, None, ALU.mult))
                    dve.wait_ge(sem("dil_in"), 48)
                    for t in range(TILES):
                        follow(t, 0)
                    keys(0)
                    dve_chain.stop()

                    def attend(hp, more):
                        for n in range(2 * RES):
                            h, r = n // RES, n % RES
                            it = hp * 8 + n
                            dve.wait_ge(sem("dil_scores"), it + 1)
                            for a, b, s, d in ((0, T, bank[B_S], r * T), (T, T + P, bank[B_S + 1][:, 0:P], RES * T), (T + P, T + 2 * P, bank[B_S + 1][:, P:2 * P], RES * T + P)):
                                g = (a > 0) + (a > T)
                                ins = nc.vector.scalar_tensor_tensor(out=logits[:, a:b], in0=dist[:, d:d + b - a], scalar=slopes[:, hp, h * GROUPS + g:h * GROUPS + g + 1],
                                                                     in1=s, op0=ALU.mult, op1=ALU.add)
                            dve_chain(ins)
                            dve_chain(nc.vector.reduce_max(stats[:, 0:1], logits, AX_X))
                            nc.vector.tensor_scalar(stats[:, 0:1], stats[:, 0:1], -1.0, None, ALU.mult).then_inc(sem("dil_max"), 1)
                            dve.wait_ge(sem("dil_turned"), it + 1)
                            nc.vector.tensor_copy(probsT[:, 0:T], bank[B_T]).then_inc(sem("dil_low"), 1)
                            if more and n:
                                for t in tiles_of(n - 1):
                                    follow(t, hp + 1)
                            dve_chain(nc.vector.reciprocal(stats[:, 2:3], stats[:, 1:2]))
                            dve.wait_ge(sem("dil_summed_v"), it + 1)
                            nc.vector.tensor_scalar(otok[:, r, h * DH:(h + 1) * DH], bank[B_O][:, 0:DH], stats[:, 2:3], None, ALU.mult).then_inc(sem("dil_o"), 1)
                        if more:
                            follow(TILES - 1, hp + 1)
                            keys(hp + 1)
                        dve.wait_ge(sem("dil_o_turned"), hp + 1)
                        nc.vector.tensor_copy(tokens(oT[:, hp, :]), by_residue(bank[B_T])).then_inc(sem("dil_oT"), 1)
                    with dve.Fori(0, PAIRS - 1) as hp:
                        dve_chain.unit(hp, 8 * 3 + NQK)
                        attend(hp, True)
                    dve_chain.end(PAIRS - 1)
                    dve_chain.begin()
                    attend(PAIRS - 1, False)
                    dve_chain.stop()

            tail = sums_ahead(hT)
            p0 = base("proj_free", KD)
            with nc.Block() as block:
                @block.sync
                def _(sp):
                    stream.issue(sp, "dil_out")

                @block.tensor
                def _(pe):
                    pe.wait_ge(sem("dil_oT"), PAIRS)
                    stream.arrived(pe, "dil_out", 0, 0)
                    w = stream.slot(0).rearrange("p (k c) -> p k c", k=PAIRS)
                    for t in range(KD):
                        if t == 7:
                            pe.wait_ge(sem("proj_free"), p0 + 1)
                        for k in range(PAIRS):
                            m = nc.tensor.matmul(bank[t % 7], w[:, k, t * P:(t + 1) * P], oT[:, k, :], start=(k == 0), stop=(k == PAIRS - 1))
                        m.then_inc(sem("dil_out_ready" if t < KD - 1 else "unit_done"), 1)
                        if t:
                            tail.sum(pe, t - 1)
                    tail.sum(pe, KD - 1)

                @block.scalar
                def _(act):
                    for k in range(KD):
                        act.wait_ge(sem("proj_free"), p0 + k + 1)
                        tail.square(act, k)

                @block.vector
                def _(dve):
                    for t in range(KD):
                        if t < KD - 1:
                            dve.wait_ge(sem("dil_out_ready"), t + 1)
                        else:
                            stream.used_up(dve, "dil_out", 0)
                        nc.vector.tensor_tensor(xT[:, t, :], xT[:, t, :], bank[t % 7], ALU.add).then_inc(sem("proj_free"), 1)

        def ffn_segments(layer, stage, w_in, w_out):
            name = f"ffn{stage}"
            for half in range(2):
                segment(f"{name}_in{half}", 2 * FTH, tile_loads(w_in, half), by_round=True, shift=2 * half)
                segment(f"{name}_out{half}", KD, down_loads(w_out, half), by_round=True, shift=2 - 2 * half)

        def mla_segments():
            def whole(w, words, k):
                g = w.rearrange("(k p) c -> p k c", p=P)
                return lambda u: [(lambda s: s[:, 0:words].rearrange("p (k c) -> p k c", k=k), g)]
            segment("mla_dq", 1, square_loads(inp["mla_w_dq_2"][0]))
            segment("mla_dkv", 1, whole(inp["mla_w_dkv_2"][0], KD * 288, KD))
            segment("mla_uv", 1, whole(inp["mla_w_uv_2"][0], 2 * D, 2))
            uq = inp["mla_w_uq_2"][0].rearrange("(k p) (u c) -> u p k c", p=P, c=192)
            uk = inp["mla_w_uk_2"][0].rearrange("(k p) (u c) -> u p k c", p=P, c=P)
            segment("mla_heads", 8, lambda u: [
                (lambda s: s[:, 0:768].rearrange("p (k c) -> p k c", k=4), uq[u]),
                (lambda s: s[:, 768:1024].rearrange("p (k c) -> p k c", k=2), uk[u])], slots=2)
            segment("mla_o", 2, square_loads(inp["mla_w_o_2"][0]))

        def hyena_segments():
            g = inp["hy_w_in_2"][0].rearrange("(k p) (t u c) -> u t p k c", p=P, t=3, c=P)
            segment("hy_in", KD, lambda u: [
                ((lambda s, t=t: s[:, t * D:(t + 1) * D].rearrange("p (k c) -> p k c", k=KD)), g[u, t]) for t in range(3)])
            segment("hy_out", 2, square_loads(inp["hy_w_out_2"][0]))

        def gdn_segments():
            g = inp["gdn_w_in"][0][:, 0:4 * D].rearrange("(k p) (t u c) -> u t p k c", p=P, t=4, c=P)
            segment("gdn_in", GH, lambda u: [
                ((lambda s, t=t: s[:, t * D:(t + 1) * D].rearrange("p (k c) -> p k c", k=KD)), g[u, t]) for t in range(4)])
            segment("gdn_out", 2, square_loads(inp["gdn_w_out"][0]))

        def dilated_segments():
            g = inp["dil_w_in"][0].rearrange("(k p) (t g u c) -> u t g p k c", p=P, t=3, g=3, c=P)
            segment("dil_in", 12, lambda r, j: [
                ((lambda s, n=n: s[:, n * D:(n + 1) * D].rearrange("p (k c) -> p k c", k=KD)), g[r, j, n]) for n in range(3)],
                slots=3, by_round=True)
            w = inp["dil_w_out"][0].rearrange("(k p) c -> p k c", p=P)
            segment("dil_out", 1, lambda u: [(lambda s: s.rearrange("p (k c) -> p k c", k=4), w)])

        gdn_segments()
        ffn_segments(0, 2, inp["ffn_w_in"][0], inp["ffn_w_out"][0])
        dilated_segments()
        ffn_segments(1, 4, inp["ffn_w_in"][1], inp["ffn_w_out"][1])
        mla_segments()
        ffn_segments(0, 6, inp["ffn_w_up_2"][0], inp["ffn_w_down_2"][0])
        hyena_segments()
        ffn_segments(1, 8, inp["ffn_w_up_2"][1], inp["ffn_w_down_2"][1])
        stream = Stream(ring, segments, [sem(f"weights_landed{j}") for j in range(SLOTS)], sem("unit_done"))

        stage_load()
        before = list(made)
        stage_gdn()
        retire(before)
        stage_ffn(2, 0)
        before = list(made)
        stage_dilated()
        retire(before)
        stage_ffn(4, 1)
        stage_mla()
        stage_ffn(6, 0, convolved=True)
        stage_hyena()
        stage_ffn(8, 1, convolved=True)
        stage_store()


def constants():
    f = np.float32
    t = np.arange(T)
    inv = (np.float32(10000.0) ** (-np.arange(0, 16, 2, dtype=f) / f(16))).astype(f)
    ar, ac = (t // 64).astype(f)[:, None] * inv, (t % 64).astype(f)[:, None] * inv
    ang = np.concatenate([ar, ar, ac, ac], axis=1).astype(f).T
    cos, sin, rot = np.ones((P, T), f), np.zeros((P, T), f), np.zeros((P, P), f)
    cos[64:96], sin[64:96] = np.cos(ang), np.sin(ang)
    for i in range(8):
        for h in (0, 16):
            rot[64 + h + 8 + i, h + i] = -1.0
            rot[64 + h + i, h + 8 + i] = 1.0
    j, i = np.arange(P)[:, None], np.arange(P)[None, :]
    tri = (j <= i).astype(f)
    levels = np.stack([((j >> (lv + 1)) == (i >> (lv + 1))) & ((i >> lv & 1) == 1) & ((j >> lv & 1) == 0) for lv in range(7)], axis=1).astype(f)
    s, far = np.arange(P), f(1e30)
    t4 = 4 * s[:, None, None] + np.arange(4)[None, :, None]
    d0 = t4 - np.arange(T)[None, None, :]
    d0 = np.where((d0 >= 0) & (d0 <= 128), d0, far).astype(f).reshape(P, 4 * T)
    gap = s[:, None] - s[None, :]
    d1 = np.where(gap >= 0, 4 * gap, far).astype(f)
    d2 = np.where((gap >= 0) & (gap % 4 == 0), 4 * gap, far).astype(f)
    slopes = (f(2.0) ** (f(-8.0) * np.arange(1, 25, dtype=f) / f(24))).astype(f).reshape(3, 4, 2)
    slopes = np.broadcast_to(-slopes.transpose(1, 2, 0).reshape(4, 6), (P, 4, 6))
    blockones = np.kron(np.eye(2), np.ones((64, 64))).astype(f)
    tt = np.linspace(0.0, 1.0, T, dtype=f)
    wt = (f(2.0 * np.pi) * np.arange(T, dtype=f) / f(T)).astype(f)
    bands = np.linspace(1e-4, 15, 16, dtype=f)
    wf = (wt[:, None] * bands).astype(f)
    z = np.concatenate([tt[:, None], np.cos(wf), -np.sin(wf)], axis=1).astype(f)
    hy_t = np.ones((P, 8, 1), f)
    hy_t[:, 0:TB, 0] = -tt.reshape(TB, P).T
    hy_t[0, TB, 0] = 0.0
    angle = np.outer(np.arange(T), 2 * np.arange(T) + 1) % (4 * T) * (np.pi / (2 * T))
    dft = np.stack([np.cos(angle), np.sin(angle)]).astype(f)
    return {
        "dil_dist": np.concatenate([d0, d1, d2], axis=1), "dil_slopes": np.ascontiguousarray(slopes), "blockones": blockones,
        "tri": tri, "levels": np.ascontiguousarray(levels),
        "hy_z": np.ascontiguousarray(z.T), "hy_t": hy_t,
        "dft": np.ascontiguousarray(dft.reshape(2, TB, P, T).transpose(2, 0, 1, 3)),
        "idft": np.ascontiguousarray((dft / f(T)).transpose(0, 2, 1).reshape(2, TB, P, T).transpose(2, 0, 1, 3)),
        "rope_cos": cos, "rope_sin": sin, "rope_rot": rot,
        "ident": np.eye(P, dtype=f),
        "ones": np.ones((P, P), f),
    }


NAMES = ["x", "norm_mix", "norm_ffn", "gdn_w_in", "gdn_conv_w", "gdn_a_log", "gdn_dt_bias", "gdn_norm_w",
         "gdn_w_out", "dil_w_in", "dil_q_norm", "dil_k_norm", "dil_w_out", "ffn_w_in", "ffn_w_out", "c_2",
         "ctx_2", "c_ctx_2", "mod_w_2", "mod_b_2", "norm_mix_g_2", "norm_ffn_g_2", "mla_w_dq_2", "mla_g_q_2",
         "mla_w_uq_2", "mla_w_dkv_2", "mla_g_kv_2", "mla_w_uk_2", "mla_w_uv_2", "mla_w_o_2", "hy_w_in_2",
         "hy_b_in_2", "hy_conv_w_2", "hy_conv_b_2", "hy_f_w1_2", "hy_f_b1_2", "hy_f_freq1_2", "hy_f_w2_2",
         "hy_f_b2_2", "hy_f_freq2_2", "hy_f_w3_2", "hy_decay_2", "hy_d_bias_2", "hy_w_out_2", "hy_b_out_2",
         "ffn_w_up_2", "ffn_conv_w_2", "ffn_conv_b_2", "ffn_w_down_2", "final_g_2"]


def kernel(**inputs):
    import numpy as _np
    import concourse.bacc as _bacc
    from concourse.bass_utils import run_bass_kernel_spmd as _run

    nc = _bacc.Bacc("TRN2", target_bir_lowering=False, num_devices=1)
    arrays, inp, const = {}, {}, {}
    for name in NAMES:
        a = _np.ascontiguousarray(inputs[name])
        arrays["in_" + name] = a
        inp[name] = nc.dram_tensor("in_" + name, a.shape, F32, kind="ExternalInput").ap()
    for name, a in constants().items():
        arrays["const_" + name] = a
        const[name] = nc.dram_tensor("const_" + name, a.shape, F32, kind="ExternalInput").ap()
    out = nc.dram_tensor("out", (1, T, D), F32, kind="ExternalOutput").ap()
    network(nc, inp, const, out)
    r = _run(nc, [arrays], core_ids=[0])
    return r.results[0]["out"]
```
